# Optimizing a Trainium2 kernel written in Bass

```python
import math
import jax, jax.numpy as jnp
from jax import lax
import numpy as np

D_MODEL = 1024
BATCH = 1
SEQ = 256
DEPTH = 2

N_MIXERS = 2
N_ATTN_LAYERS = (DEPTH + 1) // 2
N_RET_LAYERS = DEPTH // 2
NORM_EPS = 1e-6
N_NORMS = 6

D_FF = 2816

DILATED_GROUPS = ((128, 1), (512, 4), (2048, 16))
N_GROUPS = len(DILATED_GROUPS)
H_A = 16
DH_A = 64
D_A = H_A * DH_A
ATTN_IN_COLS = N_GROUPS * 3 * D_A
BLK = 64
NEG_INF = -1e30

NUM_BUCKETS = 32
REL_MAX_DISTANCE = 1024

H_R = 4
DK_R = D_MODEL // H_R
DV_R = 2 * D_MODEL // H_R
D_V = H_R * DV_R
RET_IN_COLS = 2 * H_R * DK_R + 3 * D_V
RET_CHUNK = 128
ROPE_BASE = 10000.0


def rms_norm(x, g):
    xf = x.astype(jnp.float32)
    y = xf * lax.rsqrt(jnp.mean(xf * xf, axis=-1, keepdims=True) + NORM_EPS)
    return (y * g.astype(jnp.float32)).astype(x.dtype)

def swiglu(h, w_gate, w_up, w_down):
    return (jax.nn.silu(h @ w_gate) * (h @ w_up)) @ w_down

def t5_buckets(rel):
    half = NUM_BUCKETS // 2
    max_exact = half // 2
    n = np.abs(rel)
    large = max_exact + (np.log(np.maximum(n, 1) / max_exact)
                         / np.log(REL_MAX_DISTANCE / max_exact) * (half - max_exact)).astype(np.int64)
    large = np.minimum(large, half - 1)
    return ((rel > 0) * half + np.where(n < max_exact, n, large)).astype(np.int32)

def banded_attention(q, k, v, bias, radius):
    N, L, H, dh = q.shape
    nb = -(-L // BLK)
    Lp = nb * BLK
    qb = jnp.pad(q, ((0, 0), (0, Lp - L), (0, 0), (0, 0))).reshape(N, nb, BLK, H, dh)

    def windows(t):
        tp = jnp.pad(t, ((0, 0), (BLK, Lp - L + BLK), (0, 0), (0, 0))).reshape(N, nb + 2, BLK, H, dh)
        return jnp.concatenate([tp[:, :-2], tp[:, 1:-1], tp[:, 2:]], axis=2)

    kw, vw = windows(k), windows(v)
    a = np.arange(BLK)[:, None]
    c = np.arange(3 * BLK)[None, :]
    off = c - BLK - a
    key_pos = np.arange(nb)[:, None, None] * BLK - BLK + c[None]
    valid = (np.abs(off) <= radius)[None] & (key_pos >= 0) & (key_pos < L)
    bias_blk = bias[:, np.clip(off + radius, 0, 2 * radius)].astype(jnp.float32)

    s = jnp.einsum('nbqhd,nbkhd->nbhqk', qb, kw).astype(jnp.float32) * (dh ** -0.5) + bias_blk
    s = jnp.where(valid[None, :, None], s, NEG_INF)
    smax = jnp.max(s, axis=-1, keepdims=True)
    p = jnp.exp(s - smax)
    denom = jnp.sum(p, axis=-1, keepdims=True)
    o = jnp.einsum('nbhqk,nbkhd->nbqhd', (p / denom).astype(v.dtype), vw)
    lse = (smax + jnp.log(denom))[..., 0]
    o = o.reshape(N, Lp, H, dh)[:, :L]
    lse = lse.transpose(0, 1, 3, 2).reshape(N, Lp, H)[:, :L]
    return o, lse

def dilated_group(q, k, v, bias, dilation, radius):
    B, S, H, dh = q.shape
    Ls = S // dilation

    def split(t):
        return t.reshape(B, Ls, dilation, H, dh).transpose(0, 2, 1, 3, 4).reshape(B * dilation, Ls, H, dh)

    o, lse = banded_attention(split(q), split(k), split(v), bias, radius)
    o = o.reshape(B, dilation, Ls, H, dh).transpose(0, 2, 1, 3, 4).reshape(B, S, H, dh)
    lse = lse.reshape(B, dilation, Ls, H).transpose(0, 2, 1, 3).reshape(B, S, H)
    return o, lse

def dilated_attention(h, w_in, w_out, rel_bias):
    B, S, _ = h.shape
    proj = (h @ w_in).reshape(B, S, N_GROUPS, 3, H_A, DH_A)
    outs, lses = [], []
    for g, (window, dilation) in enumerate(DILATED_GROUPS):
        radius = window // (2 * dilation)
        buckets = t5_buckets(np.arange(-radius, radius + 1) * dilation)
        bias_g = rel_bias[g * H_A:(g + 1) * H_A][:, buckets]
        o, lse = dilated_group(proj[:, :, g, 0], proj[:, :, g, 1], proj[:, :, g, 2],
                               bias_g, dilation, radius)
        outs.append(o)
        lses.append(lse)
    wts = jax.nn.softmax(jnp.stack(lses, axis=0), axis=0)
    o = jnp.einsum('gbsh,gbshd->bshd', wts.astype(h.dtype), jnp.stack(outs, axis=0))
    return o.reshape(B, S, D_A) @ w_out

def rotary(t, pos):
    half = t.shape[-1] // 2
    inv_freq = 1.0 / (ROPE_BASE ** jnp.linspace(0.0, 1.0, half, dtype=jnp.float32))
    ang = pos[:, None] * inv_freq[None, :]
    cos = jnp.cos(ang)[None, :, None, :]
    sin = jnp.sin(ang)[None, :, None, :]
    t1, t2 = t[..., :half], t[..., half:]
    return jnp.concatenate([t1 * cos - t2 * sin, t1 * sin + t2 * cos], axis=-1)

def chunk_retention(q, k, v, log_gamma):
    B, S, H, dk = q.shape
    dv = v.shape[-1]
    C = RET_CHUNK
    n = S // C

    def to_chunks(t):
        return t.reshape(B, n, C, H, t.shape[-1]).transpose(1, 0, 3, 2, 4)

    qc, kc, vc = to_chunks(q), to_chunks(k), to_chunks(v)
    i = jnp.arange(C, dtype=jnp.float32)
    rel = i[:, None] - i[None, :]
    dmat = jnp.where(rel >= 0, jnp.exp(log_gamma[:, None, None] * jnp.maximum(rel, 0.0)), 0.0)
    inner = jnp.einsum('nbhid,nbhjd->nbhij', qc, kc) * dmat
    inner = jnp.einsum('nbhij,nbhje->nbhie', inner, vc)
    q_decay = jnp.exp(log_gamma[:, None] * (i + 1.0))[None, :, :, None]
    k_decay = jnp.exp(log_gamma[:, None] * (C - 1.0 - i))[None, :, :, None]
    chunk_decay = jnp.exp(log_gamma * C)[None, :, None, None]

    def step(state, xs):
        qi, ki, vi = xs
        cross = jnp.einsum('bhid,bhde->bhie', qi, state) * q_decay
        state = state * chunk_decay + jnp.einsum('bhjd,bhje->bhde', ki * k_decay, vi)
        return state, cross

    _, cross = lax.scan(step, jnp.zeros((B, H, dk, dv), jnp.float32), (qc, kc, vc))
    y = inner + cross
    return y.transpose(1, 0, 3, 2, 4).reshape(B, S, H, dv)

def head_group_norm(y):
    mu = jnp.mean(y, axis=-1, keepdims=True)
    var = jnp.mean(jnp.square(y - mu), axis=-1, keepdims=True)
    return (y - mu) * lax.rsqrt(var + NORM_EPS)

def retention(h, w_in, w_out, decay_logit):
    B, S, _ = h.shape
    proj = (h @ w_in).astype(jnp.float32)
    dq = H_R * DK_R
    q = proj[..., :dq].reshape(B, S, H_R, DK_R)
    k = proj[..., dq:2 * dq].reshape(B, S, H_R, DK_R)
    v = proj[..., 2 * dq:2 * dq + D_V].reshape(B, S, H_R, DV_R)
    g_f = proj[..., 2 * dq + D_V:2 * dq + 2 * D_V].reshape(B, S, H_R, DV_R)
    g_b = proj[..., 2 * dq + 2 * D_V:].reshape(B, S, H_R, DV_R)
    pos = jnp.arange(S, dtype=jnp.float32)
    q = rotary(q, pos)
    k = rotary(k, pos) * (DK_R ** -0.5)
    log_gamma = jnp.log1p(-jnp.exp(decay_logit.astype(jnp.float32)))
    y_f = chunk_retention(q, k, v, log_gamma[0])
    y_b = jnp.flip(chunk_retention(jnp.flip(q, 1), jnp.flip(k, 1), jnp.flip(v, 1), log_gamma[1]), 1)
    y = jax.nn.silu(g_f) * head_group_norm(y_f) + jax.nn.silu(g_b) * head_group_norm(y_b)
    return y.reshape(B, S, D_V).astype(h.dtype) @ w_out

def first_inputs(seed: int = 0) -> dict:
    key = jax.random.key(seed)
    ks = jax.random.split(key, 12)
    f32 = jnp.float32
    x = jax.random.normal(ks[0], (BATCH, SEQ, D_MODEL), f32)
    norm_gains = 1.0 + 0.05 * jax.random.normal(ks[1], (DEPTH, N_NORMS, D_MODEL), f32)
    ffn_w_gate = jax.random.normal(ks[2], (DEPTH, 2, D_MODEL, D_FF), f32) * D_MODEL ** -0.5
    ffn_w_up = jax.random.normal(ks[3], (DEPTH, 2, D_MODEL, D_FF), f32) * D_MODEL ** -0.5
    ffn_w_down = jax.random.normal(ks[4], (DEPTH, 2, D_FF, D_MODEL), f32) * D_FF ** -0.5
    attn_w_in = jax.random.normal(ks[5], (N_ATTN_LAYERS, D_MODEL, ATTN_IN_COLS), f32) * D_MODEL ** -0.5
    attn_w_out = jax.random.normal(ks[6], (N_ATTN_LAYERS, D_A, D_MODEL), f32) * D_A ** -0.5
    rel_bias = 0.5 * jax.random.normal(ks[7], (N_GROUPS * H_A, NUM_BUCKETS), f32)
    ret_w_in = jax.random.normal(ks[8], (N_RET_LAYERS, D_MODEL, RET_IN_COLS), f32) * D_MODEL ** -0.5
    ret_w_out = jax.random.normal(ks[9], (N_RET_LAYERS, D_V, D_MODEL), f32) * D_V ** -0.5
    base = -(5.0 + jnp.arange(H_R, dtype=f32)) * math.log(2.0)
    ret_decay_logit = base[None, None, :] + 0.1 * jax.random.normal(ks[10], (N_RET_LAYERS, 2, H_R), f32)
    return {"x": x, "norm_gains": norm_gains, "ffn_w_gate": ffn_w_gate, "ffn_w_up": ffn_w_up,
            "ffn_w_down": ffn_w_down, "attn_w_in": attn_w_in, "attn_w_out": attn_w_out,
            "rel_bias": rel_bias, "ret_w_in": ret_w_in, "ret_w_out": ret_w_out,
            "ret_decay_logit": ret_decay_logit}

def first_block(x, norm_gains, ffn_w_gate, ffn_w_up, ffn_w_down, attn_w_in, attn_w_out,
              rel_bias, ret_w_in, ret_w_out, ret_decay_logit):
    for i in range(DEPTH):
        g = norm_gains[i]
        h = swiglu(rms_norm(x, g[0]), ffn_w_gate[i, 0], ffn_w_up[i, 0], ffn_w_down[i, 0])
        x = x + 0.5 * rms_norm(h, g[1])
        hm = rms_norm(x, g[2])
        if i % N_MIXERS == 0:
            j = i // N_MIXERS
            m = dilated_attention(hm, attn_w_in[j], attn_w_out[j], rel_bias)
        else:
            j = i // N_MIXERS
            m = retention(hm, ret_w_in[j], ret_w_out[j], ret_decay_logit[j])
        x = x + rms_norm(m, g[3])
        h = swiglu(rms_norm(x, g[4]), ffn_w_gate[i, 1], ffn_w_up[i, 1], ffn_w_down[i, 1])
        x = x + 0.5 * rms_norm(h, g[5])
    return x


MEM_LEN = 256
ROPE_THETA = 10000.0
EPS = 1e-6
Q_BLOCK = 128
MAX_POS_OFFSET = 4096

DIFF_HEADS = 8
DIFF_HEAD_DIM = 64
DIFF_V_DIM = 2 * DIFF_HEAD_DIM
DIFF_QK_W = DIFF_HEADS * 2 * DIFF_HEAD_DIM
DIFF_V_W = DIFF_HEADS * DIFF_V_DIM

MLA_HEADS = 8
MLA_Q_LORA = 384
MLA_KV_LORA = 256
MLA_NOPE_DIM = 64
MLA_ROPE_DIM = 32
MLA_V_DIM = 64
MLA_QK_DIM = MLA_NOPE_DIM + MLA_ROPE_DIM
MLA_V_W = MLA_HEADS * MLA_V_DIM

CROSS_HEADS = 4
CROSS_HEAD_DIM = 128
CROSS_W = CROSS_HEADS * CROSS_HEAD_DIM

N_BRANCHES = 3
D_FF_2 = 4 * D_MODEL

IN_SIZES = (DIFF_QK_W, DIFF_QK_W, DIFF_V_W, MLA_Q_LORA, MLA_KV_LORA + MLA_ROPE_DIM, CROSS_W, N_BRANCHES * D_MODEL)
IN_WIDTH = sum(IN_SIZES)


def rmsnorm(x, gain):
    xf = x.astype(jnp.float32)
    y = xf * lax.rsqrt(jnp.mean(xf * xf, axis=-1, keepdims=True) + EPS)
    return (y * gain.astype(jnp.float32)).astype(x.dtype)

def rotary_tables(positions, dim):
    inv_freq = ROPE_THETA ** (-jnp.arange(0, dim, 2, dtype=jnp.float32) / dim)
    ang = positions.astype(jnp.float32)[..., None] * inv_freq
    return jnp.cos(ang), jnp.sin(ang)

def rotary_2(x, cos, sin):
    xf = x.astype(jnp.float32)
    x1, x2 = jnp.split(xf, 2, axis=-1)
    return jnp.concatenate([x1 * cos - x2 * sin, x2 * cos + x1 * sin], axis=-1).astype(x.dtype)

def causal_block_attention(q, k, v, scale):
    B, S, H, M, Dk = q.shape
    nb = S // Q_BLOCK
    qb = q.reshape(B, nb, Q_BLOCK, H, M, Dk).transpose(1, 0, 2, 3, 4, 5)
    key_pos = jnp.arange(S)

    def one_block(args):
        q_blk, blk = args
        s = jnp.einsum('bqhmd,bkhmd->bhmqk', q_blk, k).astype(jnp.float32) * scale
        q_pos = blk * Q_BLOCK + jnp.arange(Q_BLOCK)
        mask = key_pos[None, :] <= q_pos[:, None]
        s = jnp.where(mask, s, -jnp.inf)
        p = jax.nn.softmax(s, axis=-1).astype(v.dtype)
        return jnp.einsum('bhmqk,bkhd->bqhmd', p, v)

    out = lax.map(one_block, (qb, jnp.arange(nb)))
    return out.transpose(1, 0, 2, 3, 4, 5).reshape(B, S, H, M, v.shape[-1])

def diff_attention(q, k, v, q_gain, k_gain, lam_vecs, out_gain, cos, sin, layer_idx):
    B, S, _ = q.shape
    q = q.reshape(B, S, DIFF_HEADS, 2, DIFF_HEAD_DIM)
    k = k.reshape(B, S, DIFF_HEADS, 2, DIFF_HEAD_DIM)
    v = v.reshape(B, S, DIFF_HEADS, DIFF_V_DIM)
    c, s_ = cos[:, :, None, None, :], sin[:, :, None, None, :]
    q = rotary_2(rmsnorm(q, q_gain), c, s_)
    k = rotary_2(rmsnorm(k, k_gain), c, s_)
    o = causal_block_attention(q, k, v, DIFF_HEAD_DIM ** -0.5)
    lam_init = 0.8 - 0.6 * math.exp(-0.3 * layer_idx)
    lv = lam_vecs.astype(jnp.float32)
    lam = jnp.exp(jnp.sum(lv[0] * lv[1])) - jnp.exp(jnp.sum(lv[2] * lv[3])) + lam_init
    o = o[:, :, :, 0, :] - lam.astype(o.dtype) * o[:, :, :, 1, :]
    o = rmsnorm(o, out_gain) * (1.0 - lam_init)
    return o.reshape(B, S, DIFF_V_W)

def latent_attention(c_q, c_kv_kr, qa_gain, w_qb, kva_gain, w_kvb, q_gain, k_gain, cos, sin):
    B, S, _ = c_q.shape
    q = (rmsnorm(c_q, qa_gain) @ w_qb).reshape(B, S, MLA_HEADS, MLA_QK_DIM)
    q_nope, q_rope = jnp.split(q, [MLA_NOPE_DIM], axis=-1)
    q_rope = rotary_2(q_rope, cos[:, :, None, :], sin[:, :, None, :])
    c_kv, k_rope = jnp.split(c_kv_kr, [MLA_KV_LORA], axis=-1)
    kv = (rmsnorm(c_kv, kva_gain) @ w_kvb).reshape(B, S, MLA_HEADS, MLA_NOPE_DIM + MLA_V_DIM)
    k_nope, v = jnp.split(kv, [MLA_NOPE_DIM], axis=-1)
    k_rope = rotary_2(k_rope, cos, sin)
    k_rope = jnp.broadcast_to(k_rope[:, :, None, :], (B, S, MLA_HEADS, MLA_ROPE_DIM))
    q = rmsnorm(jnp.concatenate([q_nope, q_rope], axis=-1), q_gain)
    k = rmsnorm(jnp.concatenate([k_nope, k_rope], axis=-1), k_gain)
    o = causal_block_attention(q[:, :, :, None, :], k[:, :, :, None, :], v, MLA_QK_DIM ** -0.5)
    return o.reshape(B, S, MLA_V_W)

def memory_cross_attention(q, mem_n, w_mem_kv, q_gain, k_gain):
    B, S, _ = q.shape
    q = rmsnorm(q.reshape(B, S, CROSS_HEADS, CROSS_HEAD_DIM), q_gain)
    kv = (mem_n @ w_mem_kv).reshape(B, mem_n.shape[1], 2, CROSS_HEADS, CROSS_HEAD_DIM)
    k = rmsnorm(kv[:, :, 0], k_gain)
    v = kv[:, :, 1]
    s = jnp.einsum('bshd,bmhd->bhsm', q, k).astype(jnp.float32) * (CROSS_HEAD_DIM ** -0.5)
    p = jax.nn.softmax(s, axis=-1).astype(v.dtype)
    o = jnp.einsum('bhsm,bmhd->bshd', p, v)
    return o.reshape(B, S, CROSS_W)

def second_inputs(seed: int = 0) -> dict:
    key = jax.random.key(seed)
    ks = iter(jax.random.split(key, 40))
    L = DEPTH

    def nrm(shape, fan_in, scale=1.0):
        return jax.random.normal(next(ks), shape, jnp.float32) * (scale * fan_in ** -0.5)

    def gain(shape):
        return 1.0 + 0.02 * jax.random.normal(next(ks), shape, jnp.float32)

    res_scale = (2 * DEPTH) ** -0.5
    x = jax.random.normal(next(ks), (BATCH, SEQ, D_MODEL), jnp.float32)
    mem = jax.random.normal(next(ks), (BATCH, MEM_LEN, D_MODEL), jnp.float32)
    offset = jax.random.randint(next(ks), (BATCH, 1), 0, MAX_POS_OFFSET, dtype=jnp.int32)
    positions = (offset + jnp.arange(SEQ, dtype=jnp.int32)[None, :]).astype(jnp.int32)
    return {
        "x": x,
        "mem": mem,
        "positions": positions,
        "g_mix": gain((L, D_MODEL)),
        "w_in": nrm((L, D_MODEL, IN_WIDTH), D_MODEL),
        "b_gate": 0.01 * jax.random.normal(next(ks), (L, N_BRANCHES * D_MODEL), jnp.float32),
        "diff_q_gain": gain((L, DIFF_HEAD_DIM)),
        "diff_k_gain": gain((L, DIFF_HEAD_DIM)),
        "diff_lambda": 0.1 * jax.random.normal(next(ks), (L, 4, DIFF_HEAD_DIM), jnp.float32),
        "diff_out_gain": gain((L, DIFF_V_DIM)),
        "w_diff_o": nrm((L, DIFF_V_W, D_MODEL), DIFF_V_W),
        "mla_qa_gain": gain((L, MLA_Q_LORA)),
        "w_mla_qb": nrm((L, MLA_Q_LORA, MLA_HEADS * MLA_QK_DIM), MLA_Q_LORA),
        "mla_kva_gain": gain((L, MLA_KV_LORA)),
        "w_mla_kvb": nrm((L, MLA_KV_LORA, MLA_HEADS * (MLA_NOPE_DIM + MLA_V_DIM)), MLA_KV_LORA),
        "mla_q_gain": gain((L, MLA_QK_DIM)),
        "mla_k_gain": gain((L, MLA_QK_DIM)),
        "w_mla_o": nrm((L, MLA_V_W, D_MODEL), MLA_V_W),
        "mem_gain": gain((L, D_MODEL)),
        "w_mem_kv": nrm((L, D_MODEL, 2 * CROSS_W), D_MODEL),
        "cross_q_gain": gain((L, CROSS_HEAD_DIM)),
        "cross_k_gain": gain((L, CROSS_HEAD_DIM)),
        "w_cross_o": nrm((L, CROSS_W, D_MODEL), CROSS_W),
        "w_out": nrm((L, D_MODEL, D_MODEL), D_MODEL, res_scale),
        "g_mlp": gain((L, D_MODEL)),
        "w_mlp1": nrm((L, D_MODEL, D_FF_2), D_MODEL),
        "w_mlp2": nrm((L, D_FF_2, D_MODEL), D_FF_2, res_scale),
    }

def second_block(x, mem, positions, g_mix, w_in, b_gate, diff_q_gain, diff_k_gain, diff_lambda,
              diff_out_gain, w_diff_o, mla_qa_gain, w_mla_qb, mla_kva_gain, w_mla_kvb,
              mla_q_gain, mla_k_gain, w_mla_o, mem_gain, w_mem_kv, cross_q_gain, cross_k_gain,
              w_cross_o, w_out, g_mlp, w_mlp1, w_mlp2):
    B, S, D = x.shape
    cos_d, sin_d = rotary_tables(positions, DIFF_HEAD_DIM)
    cos_r, sin_r = rotary_tables(positions, MLA_ROPE_DIM)
    split_idx = np.cumsum(IN_SIZES)[:-1].tolist()

    for l in range(DEPTH):
        h = rmsnorm(x, g_mix[l])
        dq, dk, dv, c_q, c_kv_kr, xq, gate_logits = jnp.split(h @ w_in[l], split_idx, axis=-1)

        y_diff = diff_attention(dq, dk, dv, diff_q_gain[l], diff_k_gain[l], diff_lambda[l],
                                diff_out_gain[l], cos_d, sin_d, l) @ w_diff_o[l]
        y_mla = latent_attention(c_q, c_kv_kr, mla_qa_gain[l], w_mla_qb[l], mla_kva_gain[l],
                                 w_mla_kvb[l], mla_q_gain[l], mla_k_gain[l], cos_r, sin_r) @ w_mla_o[l]
        mem_n = rmsnorm(mem, mem_gain[l])
        y_mem = memory_cross_attention(xq, mem_n, w_mem_kv[l], cross_q_gain[l], cross_k_gain[l]) @ w_cross_o[l]

        gates = jax.nn.sigmoid((gate_logits + b_gate[l]).reshape(B, S, N_BRANCHES, D))
        merged = gates[:, :, 0] * y_diff + gates[:, :, 1] * y_mla + gates[:, :, 2] * y_mem
        x = x + merged @ w_out[l]

        u = rmsnorm(x, g_mlp[l]) @ w_mlp1[l]
        x = x + jnp.square(jax.nn.relu(u)) @ w_mlp2[l]
    return x


def setup_inputs(seed=0):
    out = dict(first_inputs(seed))
    for name, value in second_inputs(seed + 1).items():
        if name != "x":
            out[name + "_2"] = value
    return out


def reference(
    x, norm_gains, ffn_w_gate, ffn_w_up, ffn_w_down, attn_w_in, attn_w_out, rel_bias, ret_w_in,
    ret_w_out, ret_decay_logit, mem_2, positions_2, g_mix_2, w_in_2, b_gate_2, diff_q_gain_2,
    diff_k_gain_2, diff_lambda_2, diff_out_gain_2, w_diff_o_2, mla_qa_gain_2, w_mla_qb_2,
    mla_kva_gain_2, w_mla_kvb_2, mla_q_gain_2, mla_k_gain_2, w_mla_o_2, mem_gain_2, w_mem_kv_2,
    cross_q_gain_2, cross_k_gain_2, w_cross_o_2, w_out_2, g_mlp_2, w_mlp1_2, w_mlp2_2,
):
    x = first_block(
        x, norm_gains, ffn_w_gate, ffn_w_up, ffn_w_down, attn_w_in, attn_w_out, rel_bias,
        ret_w_in, ret_w_out, ret_decay_logit,
    )
    return second_block(
        x, mem_2, positions_2, g_mix_2, w_in_2, b_gate_2, diff_q_gain_2, diff_k_gain_2,
        diff_lambda_2, diff_out_gain_2, w_diff_o_2, mla_qa_gain_2, w_mla_qb_2, mla_kva_gain_2,
        w_mla_kvb_2, mla_q_gain_2, mla_k_gain_2, w_mla_o_2, mem_gain_2, w_mem_kv_2,
        cross_q_gain_2, cross_k_gain_2, w_cross_o_2, w_out_2, g_mlp_2, w_mlp1_2, w_mlp2_2,
    )


_drawn_inputs = setup_inputs


def setup_inputs(seed=0):
    import zlib

    import numpy as np

    out = dict(_drawn_inputs(seed))
    spreads = {}
    factors = {'mem_2': 2.929,
     'g_mix_2': 8.0,
     'b_gate_2': 8.0,
     'diff_q_gain_2': 8.0,
     'diff_k_gain_2': 8.0,
     'diff_out_gain_2': 47.954,
     'mla_qa_gain_2': 8.0,
     'mla_kva_gain_2': 8.0,
     'mla_q_gain_2': 8.0,
     'mla_k_gain_2': 8.0,
     'mem_gain_2': 8.0,
     'w_mem_kv_2': 2.776,
     'cross_q_gain_2': 8.0,
     'cross_k_gain_2': 8.0,
     'w_cross_o_2': 2.859,
     'g_mlp_2': 6.009}
    for name, (base, spread) in spreads.items():
        noise = np.random.default_rng([zlib.crc32(name.encode()), seed]).standard_normal(out[name].shape)
        drawn = base * np.exp(spread * noise) if base else spread * noise
        out[name] = __import__('jax').numpy.asarray(drawn.astype(out[name].dtype))
    for name, factor in factors.items():
        out[name] = (out[name] * factor).astype(out[name].dtype)
    return out
```

```python
from collections import deque
import math

import numpy as np
import concourse.bass as bass
from concourse import mybir
from concourse.alu_op_type import AluOpType as ALU

F32 = mybir.dt.float32
F32R = mybir.dt.float32r
I32 = mybir.dt.int32
ACT = mybir.ActivationFunctionType
AX = mybir.AxisListType

P = 128
SEQ = 256
HALVES = SEQ // P
D = 1024
DC = D // P
EPS = 1e-6
D_FF = 2816
D_MLP = 4 * D
NEG = -1e30
GROUPS = ((128, 1), (512, 4), (2048, 16))
H_A, DH_A = 16, 64
N_BUCKETS, REL_MAX = 32, 1024
H_R, DK_R, DV_R = 4, 256, 512
DIFF_H, DIFF_D = 8, 64
MLA_H, MLA_QL, MLA_KVL, MLA_NOPE, MLA_ROPE, MLA_V = 8, 384, 256, 64, 32, 64
MLA_QK = MLA_NOPE + MLA_ROPE
CROSS_H, CROSS_D = 4, 128
THETA = 10000.0
LAYERS = 2
BLOCK = 512
TILE = 1024
REL_W = SEQ + P

IN_SIZES = dict(dq=1024, dk=1024, dv=1024, cq=MLA_QL, ckv=MLA_KVL + MLA_ROPE, xq=CROSS_H * CROSS_D, gate=3 * D)
IN_AT = dict(zip(IN_SIZES, np.cumsum([0] + list(IN_SIZES.values()))[:-1].tolist()))
SMALL = dict(diff_q_gain_2=64, diff_k_gain_2=64, diff_out_gain_2=128, mla_qa_gain_2=384, mla_kva_gain_2=256,
             mla_q_gain_2=96, mla_k_gain_2=96, cross_q_gain_2=128, cross_k_gain_2=128, diff_lambda_2=256)
SMALL_AT = dict(zip(SMALL, np.cumsum([0] + list(SMALL.values()))[:-1].tolist()))


def buckets(rel):
    half, exact = N_BUCKETS // 2, N_BUCKETS // 4
    n = np.abs(rel)
    large = exact + (np.log(np.maximum(n, 1) / exact) / np.log(REL_MAX / exact) * (half - exact)).astype(np.int64)
    large = np.minimum(large, half - 1)
    return (rel > 0) * half + np.where(n < exact, n, large)


def constants():
    dist = np.arange(REL_W)[None, :] - np.arange(P)[:, None] - P
    onehot = np.zeros((len(GROUPS), N_BUCKETS + 1, 2 * SEQ), np.float32)
    for g, (window, dil) in enumerate(GROUPS):
        for i in range(2 * SEQ - 1):
            rel = i - (SEQ - 1)
            if rel % dil == 0 and abs(rel // dil) <= window // (2 * dil):
                onehot[g, int(buckets(np.array(rel))), i] = 1.0
            else:
                onehot[g, N_BUCKETS, i] = NEG
    pos = np.arange(SEQ, dtype=np.float32)
    freq = (np.float32(1.0) / (THETA ** np.linspace(0, 1, DK_R // 2, dtype=np.float32).astype(np.float64)).astype(np.float32)).astype(np.float32)
    ang = (pos[:, None] * freq[None, :]).astype(np.float32).astype(np.float64)
    by_half = lambda t: t.astype(np.float32).reshape(HALVES, P, -1).transpose(1, 0, 2)
    ret = np.stack([by_half(np.cos(ang)), by_half(np.sin(ang))], axis=1)
    inv = [THETA ** (-np.arange(0, n, 2, dtype=np.float64) / n) for n in (DIFF_D, MLA_ROPE)]
    return dict(
        c_ident=np.eye(P, dtype=np.float32),
        c_flip=np.ascontiguousarray(np.eye(P, dtype=np.float32)[::-1]),
        c_dist=dist.astype(np.float32),
        c_causal=np.where(dist <= 0, 0.0, NEG).astype(np.float32),
        c_onehot=np.ascontiguousarray(onehot.transpose(1, 0, 2)),
        c_ret_rope=np.ascontiguousarray(ret),
        c_inv_freq=np.concatenate(inv).astype(np.float32)[None, :],
    )




class Engine:

    def __init__(self, nc, e, name):
        self.e, self.name, self.sem, self.n, self.seen = e, name, nc.alloc_semaphore("done_" + name), 0, {}

    def wait(self, *tickets):
        for t in tickets:
            if t is None:
                continue
            if isinstance(t, list):
                self.wait(*t)
            elif self.seen.get(t[2], 0) < t[1]:
                self.seen[t[2]] = t[1]
                self.e.wait_ge(t[0], t[1])

    def do(self, instruction):
        self.n += 1
        instruction.then_inc(self.sem, 1)
        return (self.sem, self.n, self.name)

    def last(self):
        return (self.sem, self.n, self.name)


class Slots:

    def __init__(self, items):
        self.free = deque((item, None) for item in items)

    def take(self):
        return self.free.popleft()

    def give(self, item, *tickets):
        self.free.append((item, list(tickets)))


class DmaSlot:

    def __init__(self, nc, name, tensor):
        self.tensor, self.name, self.sem, self.n = tensor, "dma_" + name, nc.alloc_semaphore("dma_" + name), 0

    def filled(self, dma):
        self.n += 16
        dma.then_inc(self.sem, 16)
        return (self.sem, self.n, self.name)


class Transposed:

    def __init__(self, nc, name, chunks, hi_at, lo_at):
        self.hi = nc.alloc_sbuf_tensor_at(name + "_hi", [P, HALVES, chunks, P], F32R, offset=hi_at)
        self.lo = nc.alloc_sbuf_tensor_at(name + "_lo", [P, HALVES, chunks, P], F32R, offset=lo_at)
        self.ready, self.free, self.size = {}, None, chunks * HALVES * P * 4


def pieces(w, rows, c0, n):
    chunks, per = rows // P, TILE // n
    view = w.rearrange("(k p) n -> p k n", p=P)
    return [(view[:, k:min(k + per, chunks), c0:c0 + n], min(per, chunks - k), n) for k in range(0, chunks, per)]


def column_blocks(n, start=0):
    return [(start + c, min(BLOCK, n - c)) for c in range(0, n, BLOCK)]


def weight_plan(a, stages):
    plan = []

    def mat(w, rows, n, start=0):
        for c0, m in column_blocks(n, start):
            plan.extend(pieces(w, rows, c0, m))

    for kind, i, j in stages:
        if kind == "ffn":
            for c0, m in column_blocks(D_FF):
                plan.extend(pieces(a["ffn_w_gate"][i, j], D, c0, m))
                plan.extend(pieces(a["ffn_w_up"][i, j], D, c0, m))
            mat(a["ffn_w_down"][i, j], D_FF, D)
        if kind == "dilated":
            mat(a["attn_w_in"][0], D, len(GROUPS) * 3 * D)
            mat(a["attn_w_out"][0], D, D)
        if kind == "retention":
            mat(a["ret_w_in"][0], D, 2 * D + 3 * H_R * DV_R)
            mat(a["ret_w_out"][0], H_R * DV_R, D)
        if kind == "mix":
            mat(a["w_mem_kv_2"][i], D, D)
            for part in ("cq", "ckv", "dq", "dk"):
                mat(a["w_in_2"][i], D, IN_SIZES[part], IN_AT[part])
            mat(a["w_mla_qb_2"][i], MLA_QL, MLA_H * MLA_QK)
            mat(a["w_mla_kvb_2"][i], MLA_KVL, MLA_H * (MLA_NOPE + MLA_V))
            for part in ("dv", "xq", "gate"):
                mat(a["w_in_2"][i], D, IN_SIZES[part], IN_AT[part])
            for c0, m in column_blocks(D):
                plan.extend(pieces(a["w_mla_o_2"][i], MLA_H * MLA_V, c0, m))
                plan.extend(pieces(a["w_cross_o_2"][i], CROSS_H * CROSS_D, c0, m))
                plan.extend(pieces(a["w_diff_o_2"][i], D, c0, m))
            mat(a["w_out_2"][i], D, D)
        if kind == "mlp":
            mat(a["w_mlp1_2"][i], D, D_MLP)
            mat(a["w_mlp2_2"][i], D_MLP, D)
    return plan


def gain_plan(a, stages):
    plan = []
    for kind, i, j in stages:
        if kind == "ffn":
            plan += [a["norm_gains"][i, 4 * j], a["norm_gains"][i, 4 * j + 1]]
        if kind in ("dilated", "retention"):
            plan += [a["norm_gains"][i, 2], a["norm_gains"][i, 3]]
        if kind == "mix":
            plan += [a["mem_gain_2"][i], a["g_mix_2"][i]]
            plan += [a["b_gate_2"][i, c * D:(c + 1) * D] for c in range(3)]
        if kind == "mlp":
            plan += [a["g_mlp_2"][i]]
    return plan


class WeightStream:
    RAW, SPLIT = 4, 4

    def __init__(self, nc, k, plan):
        self.k, self.plan, self.at, self.loaded, self.ready = k, plan, 0, {}, {}
        self.raw = [DmaSlot(nc, f"w{i}", k.sbuf(f"w_raw{i}", [P, TILE])) for i in range(self.RAW)]
        self.raw_free = [None] * self.RAW
        self.hi = [k.sbuf(f"w_hi{i}", [P, TILE], F32R) for i in range(self.SPLIT)]
        self.lo = [k.sbuf(f"w_lo{i}", [P, TILE], F32R) for i in range(self.SPLIT)]
        self.split_free = [None] * self.SPLIT

    def start(self):
        for i in range(min(self.RAW, len(self.plan))):
            self.load(i)
        for i in range(min(self.SPLIT, len(self.plan))):
            self.split(i)

    def load(self, i):
        view, nk, n = self.plan[i]
        slot = i % self.RAW
        self.k.sync.wait(self.raw_free[slot])
        dst = self.raw[slot].tensor[:, 0:nk * n].rearrange("p (k n) -> p k n", k=nk)
        self.loaded[i] = self.raw[slot].filled(self.k.sync.e.dma_start(dst, view))

    def split(self, i):
        _, nk, n = self.plan[i]
        act, dve = self.k.act, self.k.dve
        r, s, m = i % self.RAW, i % self.SPLIT, nk * n
        raw, hi, lo = self.raw[r].tensor[:, 0:m], self.hi[s][:, 0:m], self.lo[s][:, 0:m]
        act.wait(self.loaded.pop(i), self.split_free[s])
        t = act.do(act.e.activation(hi, raw, ACT.Copy))
        dve.wait(t)
        self.ready[i] = self.raw_free[r] = dve.do(dve.e.tensor_tensor(lo, raw, hi.bitcast(F32), ALU.subtract))
        if i + self.RAW < len(self.plan):
            self.load(i + self.RAW)

    def next(self, nk, n):
        i = self.at
        self.at += 1
        assert self.plan[i][1:] == (nk, n), (i, self.plan[i][1:], nk, n)
        return i, self.hi[i % self.SPLIT], self.lo[i % self.SPLIT], self.ready.pop(i)

    def give(self, i, ticket):
        self.split_free[i % self.SPLIT] = ticket
        if i + self.SPLIT < len(self.plan):
            self.split(i + self.SPLIT)


class GainStream:
    SLOTS = 2

    def __init__(self, nc, k, plan):
        self.k, self.plan, self.at, self.loaded = k, plan, 0, {}
        self.slot = [DmaSlot(nc, f"gain{i}", k.sbuf(f"gain{i}", [P, D])) for i in range(self.SLOTS)]

    def start(self):
        for i in range(min(self.SLOTS, len(self.plan))):
            self.load(i)

    def load(self, i):
        s = self.slot[i % self.SLOTS]
        self.loaded[i] = s.filled(self.k.pool.e.dma_start(s.tensor[:, :], self.plan[i].partition_broadcast(P)))

    def next(self):
        i = self.at
        self.at += 1
        return i, self.slot[i % self.SLOTS].tensor, self.loaded.pop(i)

    def give(self, i, *readers):
        if i + self.SLOTS < len(self.plan):
            self.k.pool.wait(*readers)
            self.load(i + self.SLOTS)


class Kernel:
    def __init__(self, nc, a, stages):
        self.nc, self.a = nc, a
        self.pe, self.act, self.dve, self.pool = (
            Engine(nc, e, n) for e, n in ((nc.tensor, "pe"), (nc.scalar, "act"), (nc.vector, "dve"), (nc.gpsimd, "pool")))
        self.sync = Engine(nc, nc.sync, "sync")
        self.top = nc.sbuf_base
        psum = nc.alloc_psum_tensor("banks", [P, 8, BLOCK], F32)
        self.banks = Slots([psum[:, b, :] for b in range(8)])
        self.weights = WeightStream(nc, self, weight_plan(a, stages))
        self.gains = GainStream(nc, self, gain_plan(a, stages))
        self.x = self.sbuf("x", [P, HALVES, D])
        self.x_ready = [None] * HALVES
        self.tok = self.sbuf("tok", [P, HALVES, D])
        self.tok_free = [None, None]
        at = self.room(2 * DC * SEQ * 4)
        self.xt = Transposed(nc, "xt", DC, at, at + DC * SEQ * 4)
        self.tmp = Slots([self.sbuf(f"tmp{i}", [P, BLOCK]) for i in range(4)])
        self.probs = Slots([self.sbuf(f"probs{i}", [P, HALVES * SEQ]) for i in range(3)])
        self.probs_t = Slots([self.sbuf(f"probs_t{i}", [P, 2, 2, P]) for i in range(2)])
        self.junk = self.sbuf("junk", [P, BLOCK], mybir.dt.bfloat16)
        self.junk_written = None
        self.stats = [self.sbuf(f"stat{i}", [P, 16]) for i in range(24)]
        self.stat_at = 0
        self.minus_half = self.sbuf("minus_half", [P, 16])
        self.ident = self.sbuf("ident", [P, P])
        self.flip_tokens = self.sbuf("flip", [P, P])
        self.causal = self.sbuf("causal", [P, REL_W])
        self.small = self.sbuf("small", [P, sum(SMALL.values())])
        self.small_dma = DmaSlot(nc, "small", None)
        self.rope = self.sbuf("rope", [P, 2, HALVES, (DIFF_D + MLA_ROPE) // 2])
        self.const_dma = DmaSlot(nc, "const", None)
        self.big = self.room(0)
        self.big_bytes = nc.sbuf_usable_end - self.big
        self.flip = 0
        self.setup(stages)

    def room(self, size):
        at = (self.top + 31) // 32 * 32
        self.top = at + size
        assert self.top <= self.nc.sbuf_usable_end
        return at

    def sbuf(self, name, shape, dtype=F32):
        return self.nc.alloc_sbuf_tensor_at(name, shape, dtype, offset=self.room(int(np.prod(shape[1:])) * (2 if dtype == mybir.dt.bfloat16 else 4)))

    def place(self, name, kib, shape, dtype=F32):
        size = int(np.prod(shape[1:])) * 4
        assert kib * 1024 + size <= self.big_bytes, (name, kib, size, self.big_bytes)
        return self.nc.alloc_sbuf_tensor_at(name, shape, dtype, offset=self.big + int(kib * 1024))

    def place_t(self, name, kib, chunks):
        at, size = self.big + int(kib * 1024), chunks * SEQ * 4
        assert kib * 1024 + 2 * size <= self.big_bytes, (name, kib)
        return Transposed(self.nc, name, chunks, at, at + size)

    def stat(self, n):
        self.stat_at += 1
        return self.stats[self.stat_at % len(self.stats)][:, 0:n]

    def setup(self, stages):
        nc, a = self.nc, self.a
        c = self.const_dma
        act = self.act
        xs = a["x"][0].rearrange("(h p) d -> p h d", p=P)
        t = c.filled(act.e.dma_start(self.x[:, :, :], xs))
        self.x_ready = [t] * HALVES
        for dst, src in ((self.ident, a["c_ident"]), (self.flip_tokens, a["c_flip"]), (self.causal, a["c_causal"])):
            t = c.filled(act.e.dma_start(dst[:, :], src))
        self.x_ready = [t] * HALVES
        self.consts = t
        self.half_set = self.dve.do(self.dve.e.memset(self.minus_half[:, :], -0.5))
        self.gains.start()
        self.weights.start()
        self.pe.wait(t)

    def turn(self, src, dst, chunks, ready, dst_free, order=None):
        pe, act, dve = self.pe, self.act, self.dve
        for half in range(HALVES):
            pe.wait(ready[half])
            for c0 in range(0, len(chunks), 4):
                some = chunks[c0:c0 + 4]
                bank, free = self.banks.take()
                pe.wait(free)
                for j, (c, s) in enumerate(some):
                    last = pe.e.transpose(bank[:, j * P:(j + 1) * P], src(half, s), (order or self.ident)[:, :])
                t = pe.do(last)
                n = len(some)
                hi, lo = (x[:, half, some[0][0]:some[0][0] + n, :] for x in (dst.hi, dst.lo))
                view = bank[:, 0:n * P].rearrange("p (c t) -> p c t", c=n)
                act.wait(t, dst_free)
                h = act.do(act.e.activation(hi, view, ACT.Copy))
                dve.wait(h)
                v = dve.do(dve.e.tensor_tensor(lo, view, hi.bitcast(F32), ALU.subtract))
                self.banks.give(bank, v)
                for c, _ in some:
                    dst.ready[half, c] = v

    def turn_all(self, src, dst, n, ready, first=0, order=None):
        self.turn(lambda half, s: src(half)[:, s * P:(s + 1) * P], dst, [(first + c, c) for c in range(n)], ready, dst.free, order)

    def block(self, xt, rows, n, first=0):
        pe = self.pe
        chunks, per = rows // P, TILE // n
        out = [self.banks.take() for _ in range(HALVES)]
        pe.wait(out[0][1], out[1][1])
        tickets = [None] * HALVES
        for k0 in range(0, chunks, per):
            nk = min(per, chunks - k0)
            i, hi, lo, ready = self.weights.next(nk, n)
            pe.wait(ready)
            for half in range(HALVES):
                bank = out[half][0][:, 0:n]
                for j in range(nk):
                    k = k0 + j
                    pe.wait(xt.ready[half, first + k])
                    ah, al = xt.hi[:, half, first + k, :], xt.lo[:, half, first + k, :]
                    wh, wl = hi[:, j * n:(j + 1) * n], lo[:, j * n:(j + 1) * n]
                    pe.e.matmul(bank, ah, wh, start=(k == 0), stop=False)
                    pe.e.matmul(bank, ah, wl, start=False, stop=False)
                    last = pe.e.matmul(bank, al, wh, start=False, stop=(k == chunks - 1))
                if k0 + nk == chunks or half == HALVES - 1:
                    tickets[half] = pe.do(last)
            self.weights.give(i, tickets[HALVES - 1])
            yield
        xt.free = tickets[HALVES - 1]
        return [b for b, _ in out], tickets

    def evacuate(self, dst, bank, ticket, free=None):
        self.flip ^= 1
        e = self.act if self.flip else self.dve
        e.wait(ticket, free)
        t = e.do(e.e.activation(dst, bank, ACT.Copy) if e is self.act else e.e.tensor_copy(dst, bank))
        return t

    def project(self, xt, rows, n, dst, free=None, first=0):
        ready = [[] for _ in range(HALVES)]
        for c0, m in column_blocks(n):
            banks, tickets = yield from self.block(xt, rows, m, first)
            for half in range(HALVES):
                t = self.evacuate(dst[:, half, c0:c0 + m], banks[half][:, 0:m], tickets[half], free)
                self.banks.give(banks[half], t)
                ready[half].append(t)
        return ready

    @staticmethod
    def drive(main, side=None, every=1):
        n = 0
        while True:
            try:
                next(main)
            except StopIteration as stop:
                result = stop.value
                break
            n += 1
            if side is not None and n % every == 0:
                next(side, None)
        if side is not None:
            for _ in side:
                pass
        return result

    def square_sum(self, src, out, ready):
        act = self.act
        act.wait(ready, self.junk_written)
        self.junk_written = act.do(act.e.activation(self.junk[:, 0:src.shape[-1]], src, ACT.Square, accum_out=out))
        return self.junk_written

    def rstd(self, total, count, ready, factor=1.0):
        dve, pool = self.dve, self.pool
        n = total.shape[-1]
        mean, out = self.stat(n), self.stat(n)
        dve.wait(ready)
        t = dve.do(dve.e.tensor_scalar(mean, total, 1.0 / (count * factor ** 2), EPS / factor ** 2, ALU.mult, ALU.add))
        pool.wait(t, self.half_set)
        return out, pool.do(pool.e.tensor_tensor(out, mean, self.minus_half[:, 0:n], ALU.pow))

    def row_rstd(self, srcs, count, ready, factor=1.0):
        sums = self.stat(len(srcs))
        ts = [self.square_sum(s, sums[:, i:i + 1], r) for i, (s, r) in enumerate(zip(srcs, ready))]
        dve = self.dve
        total = sums
        if len(srcs) > 1:
            total = self.stat(1)
            dve.wait(*ts)
            ts = [dve.do(dve.e.tensor_reduce(total, sums, AX.X, ALU.add))]
        return self.rstd(total, count, ts, factor)

    def norm(self, src, src_ready, dst, dst_free):
        dve = self.dve
        gi, gain, g_ready = self.gains.next()
        ready = []
        for half in range(HALVES):
            parts = [src[:, half, c:c + BLOCK] for c in range(0, D, BLOCK)]
            r, t = self.row_rstd(parts, D, [src_ready[half]] * 2)
            dve.wait(t, g_ready, dst_free[half])
            ready.append(dve.do(dve.e.scalar_tensor_tensor(dst[:, half, :], src[:, half, :], r, gain[:, :], ALU.mult, ALU.mult)))
        self.gains.give(gi, ready[-1])
        return ready

    def norm_x(self):
        ready = self.norm(self.x, self.x_ready, self.tok, self.tok_free)
        self.turn_all(lambda half: self.tok[:, half, :], self.xt, DC, ready)
        self.tok_free = [self.pe.last()] * HALVES

    def add_normed(self, y, factor):
        dve = self.dve
        gi, gain, g_ready = self.gains.next()
        for half in range(HALVES):
            banks = [b[half] for b, _ in y]
            ready = [t[half] for _, t in y]
            r, t = self.row_rstd(banks, D, ready, factor)
            dve.wait(t, g_ready)
            for c, bank in enumerate(banks):
                tmp, free = self.tmp.take()
                dve.wait(free, ready[c])
                cols = slice(c * BLOCK, (c + 1) * BLOCK)
                t = dve.do(dve.e.scalar_tensor_tensor(tmp[:, :], bank, r, gain[:, cols], ALU.mult, ALU.mult))
                self.banks.give(bank, t)
                dve.wait(t, self.x_ready[half])
                xs = self.x[:, half, cols]
                t = dve.do(dve.e.tensor_tensor(xs, xs, tmp[:, :], ALU.add))
                self.tmp.give(tmp, t)
            self.x_ready[half] = t
        self.gains.give(gi, t)

    def add_plain(self, y):
        dve = self.dve
        for half in range(HALVES):
            for c, (banks, tickets) in enumerate(y):
                xs = self.x[:, half, c * BLOCK:(c + 1) * BLOCK]
                dve.wait(tickets[half], self.x_ready[half])
                t = dve.do(dve.e.tensor_tensor(xs, banks[half], xs, ALU.add))
                self.banks.give(banks[half], t)
            self.x_ready[half] = t

    def two_blocks(self, xt, rows):
        out = []
        for _, m in column_blocks(D):
            out.append((yield from self.block(xt, rows, m)))
        return out

    def hidden(self, n_hidden, gated, ht):
        act, dve = self.act, self.dve
        waiting = None

        def turn_block(c0, m, h, tickets):
            chunks = [(c0 // P + j, j) for j in range(m // P)]
            self.turn(lambda half, s: h[half][:, s * P:(s + 1) * P], ht, chunks, tickets, None)
            for half in range(HALVES):
                self.tmp.give(h[half], self.pe.last())

        for c0, m in column_blocks(n_hidden):
            banks, ts = yield from self.block(self.xt, D, m)
            if gated:
                up, up_ts = yield from self.block(self.xt, D, m)
            if waiting:
                turn_block(*waiting)
            h_tiles, h_ts = [], []
            for half in range(HALVES):
                h, free = self.tmp.take()
                a = banks[half][:, 0:m]
                act.wait(ts[half], free)
                t = act.do(act.e.activation(h[:, 0:m], a, ACT.Silu if gated else ACT.Relu))
                dve.wait(t)
                if gated:
                    dve.wait(up_ts[half])
                    v = dve.do(dve.e.tensor_tensor(h[:, 0:m], up[half][:, 0:m], h[:, 0:m], ALU.mult))
                    self.banks.give(up[half], v)
                else:
                    v = dve.do(dve.e.tensor_tensor(h[:, 0:m], a, h[:, 0:m], ALU.mult))
                self.banks.give(banks[half], t, v)
                h_tiles.append(h)
                h_ts.append(v)
            waiting = (c0, m, h_tiles, h_ts)
        turn_block(*waiting)

    def ffn(self, i, j):
        self.norm_x()
        ht = self.place_t(f"ffn_ht{i}{j}", 0, D_FF // P)
        self.drive(self.hidden(D_FF, True, ht))
        y = self.drive(self.two_blocks(ht, D_FF))
        self.add_normed(y, 0.5)

    def mlp(self, i, j):
        self.norm_x()
        ht = self.place_t(f"mlp_ht{i}", 0, D_MLP // P)
        self.drive(self.hidden(D_MLP, False, ht))
        self.add_plain(self.drive(self.two_blocks(ht, D_MLP)))

    def heads_t(self, src, dst, heads, ready, free=None, order=None):
        pe = self.pe
        out = []
        for h0 in range(0, heads, 2):
            bank, bank_free = self.banks.take()
            pe.wait(bank_free, *ready)
            d = src(0, h0).shape[-1]
            n = min(2, heads - h0)
            for h in range(n):
                for half in range(HALVES):
                    at = h * SEQ + half * P
                    last = pe.e.transpose(bank[0:d, at:at + P], src(half, h0 + h), (order or self.ident)[:, :])
            t = pe.do(last)
            view = bank[0:d, 0:n * SEQ].rearrange("p (h t) -> p h t", h=n)
            t = self.evacuate(dst[0:d, h0:h0 + n, :], view, t, free)
            self.banks.give(bank, t)
            out.append(t)
        return out

    def attention(self, heads, per_bank, done):
        pe, act, dve = self.pe, self.act, self.dve
        exps, turned, out = {}, {}, None

        def scores(h):
            bank, free = self.banks.take()
            pe.wait(free, *h["ready"])
            for s in range(2):
                last = pe.e.matmul(bank[:, s * SEQ:(s + 1) * SEQ], h["q"](1 - s), h["k"], start=True, stop=True)
            t = pe.do(last)
            p, free = self.probs.take()
            view = bank.rearrange("p (s k) -> p s k", s=2)
            pv = p[:, :].rearrange("p (s k) -> p s k", s=2)
            ts = []
            if h["bias"] is not None:
                b = h["bias"]
                pair = bass.AP(b.tensor, b.offset, [list(b.ap[0]), [P, 2], [1, SEQ]])
                dve.wait(t, free, h["bias_ready"]())
                t = dve.do(dve.e.scalar_tensor_tensor(pv, view, h["scale"], pair, ALU.mult, ALU.add))
                self.banks.give(bank, t)
                h["bias_used"](t)
                dve.wait(t)
                t = dve.do(dve.e.tensor_reduce(h["nmax"], pv, AX.X, ALU.max, negate=True))
                act.wait(t)
                for s in range(2):
                    ts.append(act.do(act.e.activation(pv[:, s, :], pv[:, s, :], ACT.Exp, bias=h["nmax"][:, s:s + 1],
                                                      accum_out=h["den"][:, s:s + 1])))
            else:
                raw = self.stat(2)
                dve.wait(t)
                t = dve.do(dve.e.tensor_reduce(raw, view, AX.X, ALU.max, negate=True))
                dve.wait(t)
                t = dve.do(dve.e.tensor_scalar(h["nmax"], raw, h["scale"], None, ALU.mult))
                act.wait(t, free)
                for s in range(2):
                    ts.append(act.do(act.e.activation(pv[:, s, :], view[:, s, :], ACT.Exp, bias=h["nmax"][:, s:s + 1],
                                                      scale=h["scale"], accum_out=h["den"][:, s:s + 1])))
                self.banks.give(bank, ts[-1])
            return p, ts[-1]

        def turn_probs(p, t):
            bank, free = self.banks.take()
            pe.wait(free, t)
            for kh in range(2):
                for s in range(2):
                    last = pe.e.transpose(bank[:, (2 * kh + s) * P:(2 * kh + s + 1) * P],
                                          p[:, s * SEQ + kh * P:s * SEQ + (kh + 1) * P], self.ident[:, :])
            t = pe.do(last)
            self.probs.give(p, t)
            pt, free = self.probs_t.take()
            t = self.evacuate(pt[:, :, :, :], bank.rearrange("p (k s t) -> p k s t", k=2, s=2), t, free)
            self.banks.give(bank, t)
            return pt, t

        def values(n, h, pt, t):
            nonlocal out
            j, dv = n % per_bank, h["dv"]
            if j == 0:
                out, free = self.banks.take()
                pe.wait(free)
            pe.wait(t)
            for s in range(2):
                at = (s * per_bank + j) * dv
                for kh in range(2):
                    last = pe.e.matmul(out[:, at:at + dv], pt[:, kh, s, :], h["v"](kh), start=(kh == 0), stop=(kh == 1))
            t = pe.do(last)
            self.probs_t.give(pt, t)
            if j == per_bank - 1:
                done(out, n - j, t)

        n = len(heads)
        for i in range(n + 2):
            if i < n:
                exps[i] = scores(heads[i])
            if 0 <= i - 1 < n:
                turned[i - 1] = turn_probs(*exps.pop(i - 1))
            if i >= 2:
                values(i - 2, heads[i - 2], *turned.pop(i - 2))
            yield

    def bias_tables(self):
        nc, a, pe, act = self.nc, self.a, self.pe, self.act
        table = nc.dram_tensor("bias_by_distance", [len(GROUPS) * H_A, 2 * SEQ], F32, kind="Internal").ap()
        onehot = self.place("onehot", 16, [N_BUCKETS + 1, len(GROUPS), 2 * SEQ])
        rel = self.place("rel_bias_t", 22, [N_BUCKETS + 1, len(GROUPS) * H_A])
        rows = self.place("bias_rows", 24, [H_A, len(GROUPS), 2 * SEQ])
        dma = DmaSlot(nc, "bias_in", None)
        pool = self.pool
        pool.wait(self.x_ready)
        one = pool.do(pool.e.memset(rel[N_BUCKETS:N_BUCKETS + 1, :], 1.0))
        dma.filled(pool.e.dma_start(onehot[:, :, :], a["c_onehot"]))
        t = dma.filled(pool.e.dma_start(rel[0:N_BUCKETS, :], a["rel_bias"].rearrange("h b -> b h"), allow_slow_non_contiguous=True))
        stored = DmaSlot(nc, "bias_out", None)
        copies = []
        for g in range(len(GROUPS)):
            bank, free = self.banks.take()
            pe.wait(free, t, one)
            m = pe.do(pe.e.matmul(bank[0:H_A, :], rel[:, g * H_A:(g + 1) * H_A], onehot[:, g, :], start=True, stop=True))
            act.wait(m)
            c = act.do(act.e.activation(rows[:, g, :], bank[0:H_A, :], ACT.Copy))
            self.banks.give(bank, c)
            copies.append(c)
        pool.wait(copies)
        t = stored.filled(pool.e.dma_start(table.rearrange("(g h) r -> h g r", g=len(GROUPS)), rows[:, :, :]))
        return table, t

    def dilated(self, i, j):
        nc, dve, act, pool = self.nc, self.dve, self.act, self.pool
        table, table_ready = self.bias_tables()
        self.norm_x()
        q = self.place("da_q", 0, [P, HALVES, D])
        k = self.place("da_k", 8, [P, HALVES, D])
        qt = self.place("da_qt", 16, [P, DC, SEQ])
        kt = self.place("da_kt", 24, [P, DC, SEQ])
        vs = [self.place(f"da_v{n}", 32 + 8 * n, [P, HALVES, D]) for n in range(2)]
        outs = [self.tok] + [self.place(f"da_o{n}", 48 + 8 * n, [P, HALVES, D]) for n in range(2)]
        bias = [DmaSlot(nc, f"bias{n}", self.place(f"da_bias{n}", 64 + 1.5 * n, [P, REL_W])) for n in range(6)]
        heads_n = len(GROUPS) * H_A
        nmax = self.place("da_nmax", 73, [P, heads_n, 2])
        den = self.place("da_den", 73.5, [P, heads_n, 2])
        bias_loaded, bias_used = {}, {}

        def load_bias(n):
            s = bias[n % len(bias)]
            src = bass.AP(table.tensor, n * 2 * SEQ, [[1, P], [1, REL_W]])
            pool.wait(table_ready, bias_used.get(n - len(bias)), self.x_ready)
            bias_loaded[n] = s.filled(pool.e.dma_start(s.tensor[:, :], src))

        for n in range(len(bias)):
            load_bias(n)

        def used(n):
            def note(t):
                bias_used[n] = t
                if n + len(bias) < heads_n:
                    load_bias(n + len(bias))
            return note

        side, qk_free, over = None, None, [None] * (len(GROUPS) + 2)

        def qkv(g):
            ready = []
            for dst, free in ((q, qk_free), (k, qk_free), (vs[g % 2], over[g])):
                ready.append((yield from self.project(self.xt, D, D, dst, free)))
            return ready

        for g in range(len(GROUPS)):
            v = vs[g % 2]
            q_ready, k_ready, v_ready = self.drive(qkv(g), side, 2)
            side_done = over[g + 1] = self.pe.last()
            qts = self.heads_t(lambda half, c: q[:, half, c * P:(c + 1) * P], qt, DC, q_ready, [side_done, table_ready], self.flip_tokens)
            kts = self.heads_t(lambda half, c: k[:, half, c * P:(c + 1) * P], kt, DC, k_ready, [side_done, table_ready])
            qk_free = self.pe.last()
            heads = []
            for h in range(H_A):
                n, at = g * H_A + h, DH_A * (h % 2)
                heads.append(dict(
                    q=lambda half, c=h // 2, at=at: qt[at:at + DH_A, c, half * P:(half + 1) * P],
                    k=kt[at:at + DH_A, h // 2, :],
                    v=lambda kh, v=v, h=h: v[:, kh, h * DH_A:(h + 1) * DH_A],
                    dv=DH_A, scale=DH_A ** -0.5, bias=bias[n % len(bias)].tensor[:, :],
                    bias_ready=lambda n=n: bias_loaded[n], bias_used=used(n),
                    nmax=nmax[:, n, :], den=den[:, n, :], ready=[qts[h // 4], kts[h // 4]] + v_ready))
            o = outs[g]

            def done(bank, h0, t, o=o):
                view = bank.rearrange("p (s c) -> p s c", s=2)
                t = self.evacuate(o[:, :, h0 * DH_A:(h0 + 4) * DH_A], view, t, self.tok_free)
                self.banks.give(bank, t)
                outs_ready.append(t)

            if g == 0:
                outs_ready = []
            side = self.attention(heads, 4, done)
        for _ in side:
            pass
        top, e, tot = (self.place(f"da_{n}", 74 + 0.5 * m, [P, 3, H_A, 2]) for m, n in enumerate(("top", "e", "tot")))
        by_group = lambda z: z[:, :, :].rearrange("p (g h) s -> p g (h s)", g=3)
        flat = lambda z, g: z[:, g, :, :].rearrange("p h s -> p (h s)")
        nm = by_group(nmax)
        dve.wait(outs_ready)
        t = dve.do(dve.e.tensor_tensor(flat(top, 0), nm[:, 0, :], nm[:, 1, :], ALU.min))
        dve.wait(t)
        t = dve.do(dve.e.tensor_tensor(flat(top, 0), flat(top, 0), nm[:, 2, :], ALU.min))
        dve.wait(t)
        for g in range(3):
            t = dve.do(dve.e.tensor_tensor(flat(e, g), flat(top, 0), nm[:, g, :], ALU.subtract))
        act.wait(t)
        t = act.do(act.e.activation(e[:, :, :, :], e[:, :, :, :], ACT.Exp))
        dve.wait(t)
        t = dve.do(dve.e.tensor_tensor(tot[:, :, :, :].rearrange("p g h s -> p (g h s)"),
                                       e[:, :, :, :].rearrange("p g h s -> p (g h s)"),
                                       den[:, :, :].rearrange("p n s -> p (n s)"), ALU.mult))
        for g in range(1, 3):
            dve.wait(t)
            t = dve.do(dve.e.tensor_tensor(flat(tot, 0), flat(tot, 0), flat(tot, g), ALU.add))
        dve.wait(t)
        t = dve.do(dve.e.reciprocal(flat(tot, 0), flat(tot, 0)))
        dve.wait(t)
        for g in range(3):
            t = dve.do(dve.e.tensor_tensor(flat(e, g), flat(e, g), flat(tot, 0), ALU.mult))
        dve.wait(t)
        ready = []
        for s in range(2):
            for g in range(3):
                o = outs[g][:, s, :].rearrange("p (h d) -> p h d", d=DH_A)
                c = e[:, g, :, s:s + 1].to_broadcast([P, H_A, DH_A])
                t = dve.do(dve.e.tensor_tensor(o, o, c, ALU.mult))
            for g in range(1, 3):
                dve.wait(t)
                t = dve.do(dve.e.tensor_tensor(outs[0][:, s, :], outs[0][:, s, :], outs[g][:, s, :], ALU.add))
            ready.append(t)
        self.turn_all(lambda half: self.tok[:, 1 - half, :], self.xt, DC, ready[::-1], order=self.flip_tokens)
        self.tok_free = [self.pe.last()] * HALVES
        self.add_normed(self.drive(self.two_blocks(self.xt, D)), 1.0)

    def rotate(self, first, second, cos, sin, ready):
        dve = self.dve
        dims = [int(v) for v in first.shape[1:]]
        size = int(np.prod(dims))
        tiles = [self.tmp.take() for _ in range(3)]
        a, b, c = (self.shaped(t[:, 0:size], dims) for t, _ in tiles)
        dve.wait(ready, *[f for _, f in tiles])
        dve.do(dve.e.tensor_tensor(a, first, cos, ALU.mult))
        dve.do(dve.e.tensor_tensor(c, first, sin, ALU.mult))
        t = dve.do(dve.e.tensor_tensor(b, second, sin, ALU.mult))
        dve.wait(t)
        t = dve.do(dve.e.tensor_tensor(first, a, b, ALU.subtract))
        u = dve.do(dve.e.tensor_tensor(second, second, cos, ALU.mult))
        dve.wait(u)
        u = dve.do(dve.e.tensor_tensor(second, second, c, ALU.add))
        for t_, _ in tiles:
            self.tmp.give(t_, u)
        return u

    @staticmethod
    def shaped(ap, dims):
        if len(dims) == 1:
            return ap
        return ap.rearrange("p (a b) -> p a b", a=dims[0])

    def decays(self, rel_dist):
        nc, a, act, dve, pool = self.nc, self.a, self.act, self.dve, self.pool
        n = 2 * H_R
        w = self.place("ret_small", 66, [P, 12, n])
        dma = DmaSlot(nc, "decay", None)
        pool.wait(self.x_ready)
        dma.filled(pool.e.dma_start(rel_dist[:, :], a["c_dist"]))
        t = dma.filled(pool.e.dma_start(w[:, 0, :], a["ret_decay_logit"][0].rearrange("a h -> (a h)").partition_broadcast(P)))
        col = lambda i: w[:, i, :]

        def step(fn, out, *args):
            nonlocal t
            dve.wait(t)
            t = dve.do(fn(col(out), *args))

        act.wait(t)
        t = act.do(act.e.activation(col(1), col(0), ACT.Exp))
        step(dve.e.tensor_scalar, 2, col(1), -1.0, 2.0, ALU.mult, ALU.add)
        step(dve.e.reciprocal, 2, col(2))
        step(dve.e.tensor_tensor, 2, col(2), col(1), ALU.mult)
        step(dve.e.tensor_tensor, 3, col(2), col(2), ALU.mult)
        step(dve.e.tensor_scalar, 4, col(3), 1.0 / 13, 1.0 / 11, ALU.mult, ALU.add)
        for m in (9, 7, 5, 3, 1):
            step(dve.e.tensor_tensor, 4, col(4), col(3), ALU.mult)
            step(dve.e.tensor_scalar, 4, col(4), 1.0 / m, None, ALU.add)
        step(dve.e.tensor_tensor, 4, col(4), col(2), ALU.mult)
        step(dve.e.tensor_scalar, 4, col(4), -2.0, None, ALU.mult)
        step(dve.e.tensor_scalar, 5, col(1), -1.0, 1.0, ALU.mult, ALU.add)
        act.wait(t)
        t = act.do(act.e.activation(col(6), col(5), ACT.Ln))
        step(dve.e.tensor_scalar, 7, col(1), 0.25, None, ALU.is_lt)
        step(dve.e.tensor_scalar, 8, col(7), -1.0, 1.0, ALU.mult, ALU.add)
        step(dve.e.tensor_tensor, 4, col(4), col(7), ALU.mult)
        step(dve.e.tensor_tensor, 6, col(6), col(8), ALU.mult)
        step(dve.e.tensor_tensor, 9, col(6), col(4), ALU.add)
        tiles = []
        for direction in range(2):
            span, free = self.tmp.take()
            dve.wait(t, free)
            sign = 1.0 if direction == 0 else -1.0
            s = dve.do(dve.e.tensor_scalar(span[:, 0:REL_W], rel_dist[:, :], sign, 0.0, ALU.mult, ALU.max))
            for h in range(H_R):
                out = self.place(f"decay{direction}{h}", 68 + 1.5 * (direction * H_R + h), [P, REL_W])
                lg = w[:, 9, direction * H_R + h:direction * H_R + h + 1]
                act.wait(s, t)
                e = act.do(act.e.activation(out[:, :], span[:, 0:REL_W], ACT.Exp, scale=lg))
                dve.wait(e)
                t = dve.do(dve.e.scalar_tensor_tensor(out[:, :], rel_dist[:, :], 0.0, out[:, :],
                                                      ALU.is_ge if direction == 0 else ALU.is_le, ALU.mult))
                tiles.append(out)
            self.tmp.give(span, e)
        return tiles, t

    def retention(self, i, j):
        nc, pe, act, dve, pool = self.nc, self.pe, self.act, self.dve, self.pool
        q = self.place("re_q", 0, [P, HALVES, D])
        k = self.place("re_k", 8, [P, HALVES, D])
        qt = self.place("re_qt", 16, [P, DC, SEQ])
        kt = self.place("re_kt", 24, [P, DC, SEQ])
        v = self.place("re_v", 32, [P, HALVES, 2 * D])
        gates = [self.place("re_gf", 48, [P, HALVES, 2 * D]), self.place("re_gb", 0, [P, HALVES, 2 * D])]
        dist = self.place("re_dist", 64, [P, REL_W])
        rope = self.place("re_rope", 32, [P, 2, HALVES, DK_R // 2])
        dma = DmaSlot(nc, "ret_rope", None)
        decay, decay_ready = self.decays(dist)
        self.norm_x()
        rope_ready = dma.filled(pool.e.dma_start(rope[:, :, :, :], self.a["c_ret_rope"]))
        turned = []
        for z, zt, factor in ((q, qt, 1.0), (k, kt, DK_R ** -0.5)):
            ready = self.drive(self.project(self.xt, D, D, z))
            rot = []
            for half in range(HALVES):
                heads = z[:, half, :].rearrange("p (h two d) -> p h two d", h=H_R, two=2)
                cos, sin = (rope[:, m, half:half + 1, :].to_broadcast([P, H_R, DK_R // 2]) for m in range(2))
                t = self.rotate(heads[:, :, 0, :], heads[:, :, 1, :], cos, sin, ready[half] + [rope_ready])
                if factor != 1.0:
                    dve.wait(t)
                    t = dve.do(dve.e.tensor_scalar(z[:, half, :], z[:, half, :], factor, None, ALU.mult))
                rot.append(t)
            turned.append((z, zt, rot))
        rope_used = self.dve.last()
        v_ready = self.drive(self.project(self.xt, D, 2 * D, v, rope_used))
        qk_t = []
        for z, zt, rot in turned:
            qk_t += self.heads_t(lambda half, c, z=z: z[:, half, c * P:(c + 1) * P], zt, DC, rot)
        for gate in gates:
            for c0, m in column_blocks(2 * D):
                banks, ts = self.drive(self.block(self.xt, D, m))
                for half in range(HALVES):
                    act.wait(ts[half])
                    t = act.do(act.e.activation(gate[:, half, c0:c0 + m], banks[half], ACT.Silu))
                    self.banks.give(banks[half], t)
        gate_ready = t
        per = DK_R // P
        y_ready = [[], []]
        for h in range(H_R):
            weighted = []
            for jh in range(HALVES):
                bank, free = self.banks.take()
                pe.wait(free, qk_t)
                for c in range(per):
                    last = pe.e.matmul(bank[:, 0:SEQ], kt[:, h * per + c, jh * P:(jh + 1) * P], qt[:, h * per + c, :],
                                       start=(c == 0), stop=(c == per - 1))
                t = pe.do(last)
                both, free = self.probs.take()
                for direction in range(2):
                    dk = decay[direction * H_R + h][:, P * (1 - jh):P * (1 - jh) + SEQ]
                    dve.wait(t, free, decay_ready)
                    u = dve.do(dve.e.tensor_tensor(both[:, direction * SEQ:(direction + 1) * SEQ], bank[:, 0:SEQ], dk, ALU.mult))
                self.banks.give(bank, u)
                weighted.append((both, u))
            for half in range(HALVES):
                normed = []
                for direction in range(2):
                    bank, free = self.banks.take()
                    keys = range(0, half + 1) if direction == 0 else range(half, HALVES)
                    pe.wait(free, [w[1] for w in weighted], v_ready)
                    for n, jh in enumerate(keys):
                        at = direction * SEQ + half * P
                        last = pe.e.matmul(bank, weighted[jh][0][:, at:at + P], v[:, jh, h * DV_R:(h + 1) * DV_R],
                                           start=(n == 0), stop=(n == len(keys) - 1))
                    t = pe.do(last)
                    st, mv = self.stat(6), self.stat(2)
                    dve.wait(t)
                    u = dve.do(dve.e.bn_stats(st, bank))
                    dve.wait(u)
                    u = dve.do(dve.e.bn_aggr(mv, st))
                    r, rt = self.rstd(mv[:, 1:2], 1.0, u)
                    tmp, free = self.tmp.take()
                    dve.wait(rt, free)
                    u = dve.do(dve.e.tensor_scalar(tmp[:, :], bank, mv[:, 0:1], r, ALU.subtract, ALU.mult))
                    self.banks.give(bank, u)
                    g = gates[direction][:, half, h * DV_R:(h + 1) * DV_R]
                    dve.wait(u, gate_ready)
                    u = dve.do(dve.e.tensor_tensor(g, g, tmp[:, :], ALU.mult))
                    self.tmp.give(tmp, u)
                    normed.append(g)
                dve.wait(u)
                u = dve.do(dve.e.tensor_tensor(normed[0], normed[0], normed[1], ALU.add))
                y_ready[half].append(u)
            for both, _ in weighted:
                self.probs.give(both, pe.last())
        yt = self.place_t("re_yt", 16, 2 * D // P)
        yt.free = pe.last()
        self.turn_all(lambda half: gates[0][:, half, :], yt, 2 * D // P, y_ready)
        self.add_normed(self.drive(self.two_blocks(yt, 2 * D)), 1.0)

    def angles(self):
        a, act, dve, pool, nc = self.a, self.act, self.dve, self.pool, self.nc
        nf = (DIFF_D + MLA_ROPE) // 2
        pos_i = nc.alloc_sbuf_tensor_at("pos_i", [P, HALVES, 1], I32, offset=self.big)
        pos = self.place("pos_f", 0.25, [P, HALVES, 1])
        freq = self.place("freq", 0.5, [P, nf])
        ang = self.place("ang", 1, [P, HALVES, nf])
        turns = self.place("turns", 1.5, [P, HALVES, nf])
        red = self.place("reduced", 2, [P, HALVES, nf])
        dma = DmaSlot(nc, "angles", None)
        pool.wait(self.x_ready)
        dma.filled(pool.e.dma_start(pos_i[:, :, :], a["positions_2"].rearrange("o (h p) -> p h o", p=P), allow_slow_non_contiguous=True))
        t = dma.filled(pool.e.dma_start(freq[:, :], a["c_inv_freq"][0].partition_broadcast(P)))
        dve.wait(t)
        t = dve.do(dve.e.tensor_copy(pos[:, :, :], pos_i[:, :, :]))
        dve.wait(t)
        for half in range(HALVES):
            t = dve.do(dve.e.tensor_scalar(ang[:, half, :], freq[:, :], pos[:, half, :], None, ALU.mult))
        magic = 1.5 * 2 ** 23
        two_pi = 2 * math.pi
        parts = []
        rest = two_pi
        for bits in (9, 9, 11):
            e = math.floor(math.log2(abs(rest)))
            step = 2.0 ** (e - bits + 1)
            parts.append(math.floor(rest / step) * step)
            rest -= parts[-1]
        parts.append(float(np.float32(rest)))
        for which, shift in ((0, 0.25), (1, 0.0)):
            dve.wait(t)
            t = dve.do(dve.e.tensor_scalar(turns[:, :, :], ang[:, :, :], 1.0 / two_pi, shift, ALU.mult, ALU.add))
            dve.wait(t)
            t = dve.do(dve.e.tensor_scalar(turns[:, :, :], turns[:, :, :], magic, None, ALU.add))
            dve.wait(t)
            t = dve.do(dve.e.tensor_scalar(turns[:, :, :], turns[:, :, :], -magic, None, ALU.add))
            src = ang
            for part in parts:
                dve.wait(t)
                t = dve.do(dve.e.scalar_tensor_tensor(red[:, :, :], turns[:, :, :], -part, src[:, :, :], ALU.mult, ALU.add))
                src = red
            dve.wait(t)
            t = dve.do(dve.e.tensor_scalar(red[:, :, :], red[:, :, :], shift * two_pi, math.pi, ALU.add, ALU.min))
            dve.wait(t)
            t = dve.do(dve.e.tensor_scalar(red[:, :, :], red[:, :, :], -math.pi, None, ALU.max))
            act.wait(t)
            t = act.do(act.e.activation(self.rope[:, which, :, :], red[:, :, :], ACT.Sin))
        self.rope_ready = t

    def head_norm(self, z, heads, d, gain, ready, factor=1.0):
        act, dve = self.act, self.dve
        sums = self.stat(heads)
        per = max(1, BLOCK // d)
        if heads * d <= BLOCK:
            per = heads
        for h0 in range(0, heads, per):
            n = min(per, heads - h0)
            tmp, free = self.tmp.take()
            sq = tmp[:, 0:n * d].rearrange("p (h d) -> p h d", h=n)
            act.wait(ready, free)
            t = act.do(act.e.activation(sq, z[:, h0:h0 + n, :], ACT.Square))
            dve.wait(t)
            t = dve.do(dve.e.tensor_reduce(sums[:, h0:h0 + n], sq, AX.X, ALU.add))
            self.tmp.give(tmp, t)
        r, t = self.rstd(sums, d, t, factor)
        dve.wait(t, ready)
        rb = r.rearrange("p (h o) -> p h o", o=1).to_broadcast([P, heads, d])
        t = dve.do(dve.e.tensor_tensor(z, z, rb, ALU.mult))
        dve.wait(t, self.small_ready)
        gb = gain.rearrange("p (o d) -> p o d", o=1).to_broadcast([P, heads, d])
        return dve.do(dve.e.tensor_tensor(z, z, gb, ALU.mult))

    def wide_norm(self, z, d, gain, ready):
        r, t = self.row_rstd([z], d, [ready])
        self.dve.wait(t, self.small_ready)
        return self.dve.do(self.dve.e.scalar_tensor_tensor(z, z, r, gain, ALU.mult, ALU.mult))

    def mix(self, layer, _):
        nc, a, pe, act, dve, pool = self.nc, self.a, self.pe, self.act, self.dve, self.pool
        L = f"{layer}"
        if layer == 0:
            self.angles()
        pool.wait(self.x_ready)
        for name, n in SMALL.items():
            at = SMALL_AT[name]
            src = a[name][layer]
            if name == "diff_lambda_2":
                src = src.rearrange("a b -> (a b)")
            t = self.small_dma.filled(pool.e.dma_start(self.small[:, at:at + n], src.partition_broadcast(P)))
        self.small_ready = t
        small = lambda name: self.small[:, SMALL_AT[name]:SMALL_AT[name] + SMALL[name]]
        lam_init = 0.8 - 0.6 * math.exp(-0.3 * layer)
        lam = self.place("lam" + L, 88, [P, 8])
        lv = small("diff_lambda_2").rearrange("p (a two d) -> p a two d", a=2, two=2)
        tmp, free = self.tmp.take()
        prod = tmp[:, 0:2 * DIFF_D].rearrange("p (a d) -> p a d", a=2)
        dve.wait(free, t, self.x_ready)
        t = dve.do(dve.e.tensor_tensor(prod, lv[:, :, 0, :], lv[:, :, 1, :], ALU.mult))
        dve.wait(t)
        t = dve.do(dve.e.tensor_reduce(lam[:, 0:2], prod, AX.X, ALU.add))
        self.tmp.give(tmp, t)
        act.wait(t)
        t = act.do(act.e.activation(lam[:, 2:4], lam[:, 0:2], ACT.Exp))
        dve.wait(t)
        t = dve.do(dve.e.tensor_tensor(lam[:, 4:5], lam[:, 2:3], lam[:, 3:4], ALU.subtract))
        dve.wait(t)
        lam_ready = dve.do(dve.e.tensor_scalar(lam[:, 5:6], lam[:, 4:5], lam_init, None, ALU.add))

        q = self.place("mx_q" + L, 0, [P, HALVES, D])
        k = self.place("mx_k" + L, 8, [P, HALVES, D])
        low_t = self.place_t("mx_low_t" + L, 16, (MLA_QL + MLA_KVL) // P)
        mq = self.place("mx_mq" + L, 26, [P, HALVES, MLA_H * MLA_QK])
        gates = self.place("mx_gates" + L, 8, [P, HALVES, 3 * D])
        o_diff = self.place("mx_o_diff" + L, 0, [P, HALVES, D])
        v = self.place("mx_v" + L, 32, [P, HALVES, D])
        mem_n = self.place("mx_mem_n" + L, 32, [P, HALVES, D])
        mem = self.place("mx_mem" + L, 40, [P, HALVES, D])
        qt = self.place("mx_qt" + L, 40, [P, DC, SEQ])
        kt = self.place("mx_kt" + L, 48, [P, DC, SEQ])
        kv = self.place("mx_kv" + L, 56, [P, HALVES, MLA_H * (MLA_NOPE + MLA_V)])
        mem_t = self.place_t("mx_mem_t" + L, 64, DC)
        mqt = self.place("mx_mqt" + L, 64, [P, MLA_H, SEQ])
        mkt = self.place("mx_mkt" + L, 72, [P, MLA_H, SEQ])
        mc_t = self.place_t("mx_mc_t" + L, 64, DC)
        ckt = self.place("mx_ckt" + L, 80, [P, CROSS_H, SEQ])
        cv = self.place("mx_cv" + L, 84, [P, HALVES, CROSS_H * CROSS_D])
        ck = self.place("mx_ck" + L, 0, [P, HALVES, CROSS_H * CROSS_D])
        xq = self.place("mx_xq" + L, 16, [P, HALVES, CROSS_H * CROSS_D])
        cq_cols, ckv_at = slice(0, MLA_QL), D - MLA_KVL - MLA_ROPE
        kcat = self.tok[:, :, 0:MLA_H * MLA_QK]
        o_mla, o_cross = self.tok[:, :, 0:MLA_H * MLA_V], self.tok[:, :, MLA_H * MLA_V:D]
        cqt = self.place("mx_cqt" + L, 0, [P, CROSS_H, SEQ])

        mem_dma = DmaSlot(nc, "mem" + L, None)
        t = mem_dma.filled(pool.e.dma_start(mem[:, :, :], a["mem_2"][0].rearrange("(h p) d -> p h d", p=P)))
        ready = self.norm(mem, [t, t], mem_n, [None, None])
        self.turn_all(lambda half: mem_n[:, half, :], mem_t, DC, ready)
        ck_ready = self.drive(self.project(mem_t, D, D // 2, ck))
        cv_ready = self.drive(self.project(mem_t, D, D // 2, cv))
        for half in range(HALVES):
            z = ck[:, half, :].rearrange("p (h d) -> p h d", h=CROSS_H)
            ck_ready[half] = self.head_norm(z, CROSS_H, CROSS_D, small("cross_k_gain_2"), ck_ready[half])
        ckt_ready = self.heads_t(lambda half, c: ck[:, half, c * P:(c + 1) * P], ckt, CROSS_H, ck_ready)
        ck_used = pe.last()

        self.norm_x()
        low = self.tok
        cq_ready = self.drive(self.project(self.xt, D, MLA_QL, low[:, :, 0:MLA_QL], self.tok_free))
        ckv_ready = self.drive(self.project(self.xt, D, MLA_KVL + MLA_ROPE, low[:, :, ckv_at:D], self.tok_free))
        kr = ckv_at + MLA_KVL
        rope = lambda which, half, lo, n, heads: self.rope[:, which, half:half + 1, lo:lo + n].to_broadcast([P, heads, n])
        kr_ready = [None, None]

        def low_norms():
            for half in range(HALVES):
                cq_ready[half] = self.wide_norm(low[:, half, 0:MLA_QL], MLA_QL, small("mla_qa_gain_2"), cq_ready[half])
                yield
                r = self.wide_norm(low[:, half, ckv_at:kr], MLA_KVL, small("mla_kva_gain_2"), ckv_ready[half])
                yield
                z = low[:, half:half + 1, kr:kr + MLA_ROPE]
                n = MLA_ROPE // 2
                kr_ready[half] = self.rotate(z[:, :, 0:n], z[:, :, n:2 * n], rope(0, half, DIFF_D // 2, n, 1), rope(1, half, DIFF_D // 2, n, 1),
                                             [ckv_ready[half], self.rope_ready])
                ckv_ready[half] = r
                yield

        def qk():
            dq = yield from self.project(self.xt, D, D, q)
            dk = yield from self.project(self.xt, D, D, k)
            return dq, dk

        q_ready, k_ready = self.drive(qk(), low_norms(), 1)
        self.turn_all(lambda half: low[:, half, 0:MLA_QL], low_t, MLA_QL // P, cq_ready)
        self.turn_all(lambda half: low[:, half, ckv_at:kr], low_t, MLA_KVL // P, ckv_ready, first=MLA_QL // P)

        def diff_norms():
            for z, ready, gain in ((q, q_ready, "diff_q_gain_2"), (k, k_ready, "diff_k_gain_2")):
                for half in range(HALVES):
                    heads = z[:, half, :].rearrange("p (h d) -> p h d", d=DIFF_D)
                    ready[half] = self.head_norm(heads, 2 * DIFF_H, DIFF_D, small(gain), ready[half])
                    yield
                    n = DIFF_D // 2
                    ready[half] = self.rotate(heads[:, :, 0:n], heads[:, :, n:], rope(0, half, 0, n, 2 * DIFF_H), rope(1, half, 0, n, 2 * DIFF_H),
                                              [ready[half], self.rope_ready])
                    yield

        def more():
            mq_ready = yield from self.project(low_t, MLA_QL, MLA_H * MLA_QK, mq)
            kv_ready = yield from self.project(low_t, MLA_KVL, MLA_H * (MLA_NOPE + MLA_V), kv, first=MLA_QL // P)
            v_ready = yield from self.project(self.xt, D, D, v)
            xq_ready = yield from self.project(self.xt, D, CROSS_H * CROSS_D, xq, low_t.free)
            return mq_ready, kv_ready, v_ready, xq_ready

        mq_ready, kv_ready, v_ready, xq_ready = self.drive(more(), diff_norms(), 1)
        qt_ready = self.heads_t(lambda half, c: q[:, half, c * P:(c + 1) * P], qt, DC, q_ready)
        kt_ready = self.heads_t(lambda half, c: k[:, half, c * P:(c + 1) * P], kt, DC, k_ready)
        q_used = pe.last()

        per_kv = MLA_NOPE + MLA_V
        n_heads = 2 * DIFF_H + MLA_H + CROSS_H
        nmax = self.place("mx_nmax" + L, 88.125, [P, n_heads, 2])
        den = self.place("mx_den" + L, 88.375, [P, n_heads, 2])
        mqt_ready, mkt_ready, cqt_ready = [], [], []

        def prepare():
            n = MLA_ROPE // 2
            kcat_ready = [None, None]
            for half in range(HALVES):
                z = mq[:, half, :].rearrange("p (h d) -> p h d", d=MLA_QK)
                t = self.rotate(z[:, :, MLA_NOPE:MLA_NOPE + n], z[:, :, MLA_NOPE + n:], rope(0, half, DIFF_D // 2, n, MLA_H),
                                rope(1, half, DIFF_D // 2, n, MLA_H), [mq_ready[half], self.rope_ready])
                mq_ready[half] = self.head_norm(z, MLA_H, MLA_QK, small("mla_q_gain_2"), [t, mq_ready[half]])
                yield
                zk = kcat[:, half, :].rearrange("p (h d) -> p h d", d=MLA_QK)
                dve.wait(kv_ready[half], kr_ready[half])
                dve.do(dve.e.tensor_copy(zk[:, :, 0:MLA_NOPE], kv[:, half, :].rearrange("p (h d) -> p h d", d=per_kv)[:, :, 0:MLA_NOPE]))
                t = dve.do(dve.e.tensor_copy(zk[:, :, MLA_NOPE:], low[:, half:half + 1, kr:kr + MLA_ROPE].to_broadcast([P, MLA_H, MLA_ROPE])))
                kcat_ready[half] = self.head_norm(zk, MLA_H, MLA_QK, small("mla_k_gain_2"), t)
                yield
                z = xq[:, half, :].rearrange("p (h d) -> p h d", h=CROSS_H)
                xq_ready[half] = self.head_norm(z, CROSS_H, CROSS_D, small("cross_q_gain_2"), xq_ready[half])
                yield
            cqt_ready.extend(self.heads_t(lambda half, c: xq[:, half, c * P:(c + 1) * P], cqt, CROSS_H, xq_ready, q_used))
            yield
            mqt_ready.extend(self.heads_t(lambda half, h: mq[:, half, h * MLA_QK:(h + 1) * MLA_QK], mqt, MLA_H, mq_ready, mem_t.free))
            yield
            mkt_ready.extend(self.heads_t(lambda half, h: kcat[:, half, h * MLA_QK:(h + 1) * MLA_QK], mkt, MLA_H, kcat_ready, mem_t.free))

        self.drive(iter(()), prepare())
        prepared = pe.last()
        o_ready = {"cross": [], "mla": [], "diff": []}

        def heads_of(kind):
            if kind == "cross":
                for h in range(CROSS_H):
                    yield dict(q=lambda half, h=h: cqt[:, h, half * P:(half + 1) * P], k=ckt[:, h, :],
                               v=lambda kh, h=h: cv[:, kh, h * CROSS_D:(h + 1) * CROSS_D], dv=CROSS_D, scale=CROSS_D ** -0.5,
                               bias=None, ready=[cqt_ready, ckt_ready, cv_ready], at=2 * DIFF_H + MLA_H + h)
            if kind == "mla":
                for h in range(MLA_H):
                    yield dict(q=lambda half, h=h: mqt[0:MLA_QK, h, half * P:(half + 1) * P], k=mkt[0:MLA_QK, h, :],
                               v=lambda kh, h=h: kv[:, kh, h * per_kv + MLA_NOPE:(h + 1) * per_kv], dv=MLA_V, scale=MLA_QK ** -0.5,
                               bias=self.causal[:, :], ready=[mqt_ready, mkt_ready, kv_ready], at=2 * DIFF_H + h)
            if kind == "diff":
                for h in range(DIFF_H):
                    for m in range(2):
                        r = slice(m * DIFF_D, (m + 1) * DIFF_D)
                        yield dict(q=lambda half, h=h, r=r: qt[r, h, half * P:(half + 1) * P], k=kt[r, h, :],
                                   v=lambda kh, h=h: v[:, kh, h * 2 * DIFF_D:(h + 1) * 2 * DIFF_D], dv=2 * DIFF_D, scale=DIFF_D ** -0.5,
                                   bias=self.causal[:, :], ready=[qt_ready, kt_ready, v_ready], at=2 * h + m)

        def attend(kind, per_bank, done):
            heads = list(heads_of(kind))
            for h in heads:
                h["nmax"], h["den"] = nmax[:, h["at"], :], den[:, h["at"], :]
                h["bias_ready"], h["bias_used"] = (lambda: None), (lambda t: None)
            return self.attention(heads, per_bank, done)

        def divided(kind, dst, dv, per_bank, first):
            def done(bank, h0, t):
                r = self.stat(2 * per_bank)
                rv = r.rearrange("p (s h) -> p s h", s=2)
                dve.wait(t)
                dve.wait(act.last())
                u = dve.do(dve.e.reciprocal(rv, den[:, first + h0:first + h0 + per_bank, :].rearrange("p h s -> p s h")))
                dve.wait(u)
                view = bank.rearrange("p (s h d) -> p s h d", s=2, h=per_bank)
                out = dst[:, :, h0 * dv:(h0 + per_bank) * dv].rearrange("p s (h d) -> p s h d", h=per_bank)
                rb = r.rearrange("p (s h o) -> p s h o", s=2, o=1).to_broadcast([P, 2, per_bank, dv])
                u = dve.do(dve.e.tensor_tensor(out, view, rb, ALU.mult))
                self.banks.give(bank, u)
                o_ready[kind].append(u)
            return done

        def diff_done(bank, h0, t):
            r = self.stat(4)
            rv = r.rearrange("p (s m) -> p s m", s=2)
            dve.wait(t, act.last())
            u = dve.do(dve.e.reciprocal(rv, den[:, h0:h0 + 2, :].rearrange("p m s -> p s m")))
            dve.wait(u, lam_ready)
            u = dve.do(dve.e.tensor_scalar(rv[:, :, 1:2], rv[:, :, 1:2], lam[:, 5:6], None, ALU.mult))
            tmp, free = self.tmp.take()
            dve.wait(u, free)
            view = bank.rearrange("p (s m d) -> p s m d", s=2, m=2)
            tv = tmp[:, :].rearrange("p (s m d) -> p s m d", s=2, m=2)
            rb = r.rearrange("p (s m o) -> p s m o", s=2, o=1).to_broadcast([P, 2, 2, 2 * DIFF_D])
            u = dve.do(dve.e.tensor_tensor(tv, view, rb, ALU.mult))
            self.banks.give(bank, u)
            dve.wait(u)
            c = (h0 // 2) * 2 * DIFF_D
            u = dve.do(dve.e.tensor_tensor(o_diff[:, :, c:c + 2 * DIFF_D], tv[:, :, 0, :], tv[:, :, 1, :], ALU.subtract))
            self.tmp.give(tmp, u)
            o_ready["diff"].append(u)

        def attentions():
            yield from attend("cross", 2, divided("cross", o_cross, CROSS_D, 2, 2 * DIFF_H + MLA_H))
            yield from attend("mla", 4, divided("mla", o_mla, MLA_V, 4, 2 * DIFF_H))
            yield from attend("diff", 2, diff_done)

        def gate_logits():
            for c in range(3):
                gi, b, b_ready = self.gains.next()
                for c0, m in column_blocks(D):
                    banks, ts = yield from self.block(self.xt, D, m)
                    for half in range(HALVES):
                        dve.wait(ts[half], b_ready, prepared)
                        t = dve.do(dve.e.tensor_tensor(gates[:, half, c * D + c0:c * D + c0 + m], banks[half], b[:, c0:c0 + m], ALU.add))
                        self.banks.give(banks[half], t)
                self.gains.give(gi, t)
            return t

        t = self.drive(gate_logits(), attentions(), 1)
        act.wait(t)
        for half in range(HALVES):
            gates_ready = act.do(act.e.activation(gates[:, half, :], gates[:, half, :], ACT.Sigmoid))

        for s in range(2):
            z = o_diff[:, s, :].rearrange("p (h d) -> p h d", h=DIFF_H)
            t = self.head_norm(z, DIFF_H, 2 * DIFF_D, small("diff_out_gain_2"), o_ready["diff"], 1.0 - lam_init)
            o_ready[s] = t
        mc_t.free = pe.last()
        self.turn_all(lambda half: o_mla[:, 1 - half, :], mc_t, 4, [o_ready["mla"]] * 2)
        self.turn_all(lambda half: o_cross[:, 1 - half, :], mc_t, 4, [o_ready["cross"]] * 2, first=4)
        self.turn_all(lambda half: o_diff[:, 1 - half, :], self.xt, DC, [o_ready[1], o_ready[0]])
        outputs_turned = pe.last()
        merged_ready = [None, None]
        for c0, m in column_blocks(D):
            ys = [(1, self.drive(self.block(mc_t, MLA_H * MLA_V, m))),
                  (2, self.drive(self.block(mc_t, CROSS_H * CROSS_D, m, 4))),
                  (0, self.drive(self.block(self.xt, D, m)))]
            for half in range(HALVES):
                total = self.tok[:, half, c0:c0 + m]
                for n, (g, (banks, ts)) in enumerate(ys):
                    gate = gates[:, half, g * D + c0:g * D + c0 + m]
                    dve.wait(ts[half], gates_ready, outputs_turned)
                    if n == 0:
                        t = dve.do(dve.e.tensor_tensor(total, banks[half], gate, ALU.mult))
                        self.banks.give(banks[half], t)
                        continue
                    tmp, free = self.tmp.take()
                    dve.wait(free)
                    u = dve.do(dve.e.tensor_tensor(tmp[:, 0:m], banks[half], gate, ALU.mult))
                    self.banks.give(banks[half], u)
                    dve.wait(t, u)
                    t = dve.do(dve.e.tensor_tensor(total, total, tmp[:, 0:m], ALU.add))
                    self.tmp.give(tmp, t)
                merged_ready[half] = t
        self.turn_all(lambda half: self.tok[:, half, :], self.xt, DC, merged_ready)
        self.tok_free = [pe.last()] * HALVES
        self.add_plain(self.drive(self.two_blocks(self.xt, D)))

    def store(self, out):
        dma = DmaSlot(self.nc, "out", None)
        self.sync.wait(self.x_ready)
        for half in range(HALVES):
            t = dma.filled(self.sync.e.dma_start(out[0, half * P:(half + 1) * P, :], self.x[:, half, :]))
        self.sync.wait(t)


STAGES = [("ffn", 0, 0), ("dilated", 0, 0), ("ffn", 0, 1), ("ffn", 1, 0), ("retention", 1, 0), ("ffn", 1, 1),
          ("mix", 0, 0), ("mlp", 0, 0), ("mix", 1, 0), ("mlp", 1, 0)]


def program(nc, a, out, stages=STAGES):
    k = Kernel(nc, a, stages)
    for kind, i, j in stages:
        dict(ffn=k.ffn, mlp=k.mlp, dilated=k.dilated, retention=k.retention, mix=k.mix)[kind](i, j)
    k.store(out)


INPUTS = ["x", "norm_gains", "ffn_w_gate", "ffn_w_up", "ffn_w_down", "attn_w_in", "attn_w_out", "rel_bias", "ret_w_in",
          "ret_w_out", "ret_decay_logit", "mem_2", "positions_2", "g_mix_2", "w_in_2", "b_gate_2", "diff_q_gain_2",
          "diff_k_gain_2", "diff_lambda_2", "diff_out_gain_2", "w_diff_o_2", "mla_qa_gain_2", "w_mla_qb_2",
          "mla_kva_gain_2", "w_mla_kvb_2", "mla_q_gain_2", "mla_k_gain_2", "w_mla_o_2", "mem_gain_2", "w_mem_kv_2",
          "cross_q_gain_2", "cross_k_gain_2", "w_cross_o_2", "w_out_2", "g_mlp_2", "w_mlp1_2", "w_mlp2_2"]


def kernel(**inputs):
    import concourse.bacc as bacc
    from concourse.bass_utils import run_bass_kernel_spmd

    nc = bacc.Bacc("TRN2", target_bir_lowering=False, num_devices=1)
    arrays = {name: np.ascontiguousarray(inputs[name]) for name in INPUTS}
    arrays.update(constants())
    aps, sent = {}, {}
    for name, v in arrays.items():
        sent["in_" + name] = v
        aps[name] = nc.dram_tensor("in_" + name, v.shape, mybir.dt.from_np(v.dtype), kind="ExternalInput").ap()
    out = nc.dram_tensor("out_x", (1, SEQ, D), F32, kind="ExternalOutput").ap()
    program(nc, aps, out)
    r = run_bass_kernel_spmd(nc, [sent], core_ids=[0])
    return r.results[0]["out_x"]
```

```python
from collections import deque
import math

import numpy as np
import concourse.bass as bass
from concourse import mybir
from concourse.alu_op_type import AluOpType as ALU

F32 = mybir.dt.float32
F32R = mybir.dt.float32r
I32 = mybir.dt.int32
ACT = mybir.ActivationFunctionType
AX = mybir.AxisListType

P = 128
SEQ = 256
HALVES = SEQ // P
D = 1024
DC = D // P
EPS = 1e-6
D_FF = 2816
D_MLP = 4 * D
NEG = -1e30
GROUPS = ((128, 1), (512, 4), (2048, 16))
H_A, DH_A = 16, 64
N_BUCKETS, REL_MAX = 32, 1024
H_R, DK_R, DV_R = 4, 256, 512
DIFF_H, DIFF_D = 8, 64
MLA_H, MLA_QL, MLA_KVL, MLA_NOPE, MLA_ROPE, MLA_V = 8, 384, 256, 64, 32, 64
MLA_QK = MLA_NOPE + MLA_ROPE
CROSS_H, CROSS_D = 4, 128
THETA = 10000.0
LAYERS = 2
BLOCK = 512
TILE = 1024
REL_W = SEQ + P

IN_SIZES = dict(dq=1024, dk=1024, dv=1024, cq=MLA_QL, ckv=MLA_KVL + MLA_ROPE, xq=CROSS_H * CROSS_D, gate=3 * D)
IN_AT = dict(zip(IN_SIZES, np.cumsum([0] + list(IN_SIZES.values()))[:-1].tolist()))
SMALL = dict(diff_q_gain_2=64, diff_k_gain_2=64, diff_out_gain_2=128, mla_qa_gain_2=384, mla_kva_gain_2=256,
             mla_q_gain_2=96, mla_k_gain_2=96, cross_q_gain_2=128, cross_k_gain_2=128, diff_lambda_2=256)
SMALL_AT = dict(zip(SMALL, np.cumsum([0] + list(SMALL.values()))[:-1].tolist()))


def buckets(rel):
    half, exact = N_BUCKETS // 2, N_BUCKETS // 4
    n = np.abs(rel)
    large = exact + (np.log(np.maximum(n, 1) / exact) / np.log(REL_MAX / exact) * (half - exact)).astype(np.int64)
    large = np.minimum(large, half - 1)
    return (rel > 0) * half + np.where(n < exact, n, large)


def constants():
    dist = np.arange(REL_W)[None, :] - np.arange(P)[:, None] - P
    onehot = np.zeros((len(GROUPS), N_BUCKETS + 1, 2 * SEQ), np.float32)
    for g, (window, dil) in enumerate(GROUPS):
        for i in range(2 * SEQ - 1):
            rel = i - (SEQ - 1)
            if rel % dil == 0 and abs(rel // dil) <= window // (2 * dil):
                onehot[g, int(buckets(np.array(rel))), i] = 1.0
            else:
                onehot[g, N_BUCKETS, i] = NEG
    pos = np.arange(SEQ, dtype=np.float32)
    freq = (np.float32(1.0) / (THETA ** np.linspace(0, 1, DK_R // 2, dtype=np.float32).astype(np.float64)).astype(np.float32)).astype(np.float32)
    ang = (pos[:, None] * freq[None, :]).astype(np.float32).astype(np.float64)
    by_half = lambda t: t.astype(np.float32).reshape(HALVES, P, -1).transpose(1, 0, 2)
    ret = np.stack([by_half(np.cos(ang)), by_half(np.sin(ang))], axis=1)
    inv = [THETA ** (-np.arange(0, n, 2, dtype=np.float64) / n) for n in (DIFF_D, MLA_ROPE)]
    return dict(
        c_ident=np.eye(P, dtype=np.float32),
        c_flip=np.ascontiguousarray(np.eye(P, dtype=np.float32)[::-1]),
        c_dist=dist.astype(np.float32),
        c_causal=np.where(np.concatenate([dist[:, 0:SEQ], dist[:, P:SEQ]], 1) <= 0, 0.0, NEG).astype(np.float32),
        c_onehot=np.ascontiguousarray(onehot.transpose(1, 0, 2)),
        c_ret_rope=np.ascontiguousarray(ret),
        c_inv_freq=np.concatenate(inv).astype(np.float32)[None, :],
    )




class Engine:

    def __init__(self, nc, e, name):
        self.e, self.name, self.sem, self.n, self.seen = e, name, nc.alloc_semaphore("done_" + name), 0, {}

    def wait(self, *tickets):
        for t in tickets:
            if t is None:
                continue
            if isinstance(t, list):
                self.wait(*t)
            elif self.seen.get(t[2], 0) < t[1]:
                self.seen[t[2]] = t[1]
                self.e.wait_ge(t[0], t[1])

    def do(self, instruction):
        self.n += 1
        instruction.then_inc(self.sem, 1)
        return (self.sem, self.n, self.name)

    def last(self):
        return (self.sem, self.n, self.name)


class Slots:

    def __init__(self, items):
        self.free = deque((item, None) for item in items)

    def take(self):
        return self.free.popleft()

    def give(self, item, *tickets):
        self.free.append((item, list(tickets)))


class DmaSlot:

    def __init__(self, nc, name, tensor):
        self.tensor, self.name, self.sem, self.n = tensor, "dma_" + name, nc.alloc_semaphore("dma_" + name), 0

    def filled(self, dma):
        self.n += 16
        dma.then_inc(self.sem, 16)
        return (self.sem, self.n, self.name)


class Transposed:

    def __init__(self, nc, name, chunks, hi_at, lo_at):
        self.hi = nc.alloc_sbuf_tensor_at(name + "_hi", [P, HALVES, chunks, P], F32R, offset=hi_at)
        self.lo = nc.alloc_sbuf_tensor_at(name + "_lo", [P, HALVES, chunks, P], F32R, offset=lo_at)
        self.ready, self.free = {}, None
        self.scale = [(None, None)] * HALVES

    def at(self, half, k):
        return self.hi[:, half, k, :], self.lo[:, half, k, :]


class Joined:

    def __init__(self, parts, n):
        self.parts, self.n, self.free, self.ready = parts, n, None, {}

    def at(self, half, k):
        return self.parts[k // self.n].at(half, k % self.n)

    def note(self, p):
        for (half, c), t in self.parts[p].ready.items():
            self.ready[half, p * self.n + c] = t


def pieces(w, rows, c0, n):
    chunks, per = rows // P, TILE // n
    view = w.rearrange("(k p) n -> p k n", p=P)
    return [(view[:, k:min(k + per, chunks), c0:c0 + n], min(per, chunks - k), n) for k in range(0, chunks, per)]


def rows_of(w, rows):
    view = w.rearrange("(k p) n -> p k n", p=P)
    return [(view[:, k:k + 1, :], 1, D) for k in range(rows // P)]


def column_blocks(n, start=0):
    return [(start + c, min(BLOCK, n - c)) for c in range(0, n, BLOCK)]


def weight_plan(a, stages):
    plan = []

    def mat(w, rows, n, start=0):
        for c0, m in column_blocks(n, start):
            plan.extend(pieces(w, rows, c0, m))

    for kind, i, j in stages:
        if kind == "ffn":
            for c0, m in column_blocks(D_FF):
                plan.extend(pieces(a["ffn_w_gate"][i, j], D, c0, m))
                plan.extend(pieces(a["ffn_w_up"][i, j], D, c0, m))
            mat(a["ffn_w_down"][i, j], D_FF, D)
        if kind == "dilated":
            mat(a["attn_w_in"][0], D, len(GROUPS) * 3 * D)
            plan.extend(rows_of(a["attn_w_out"][0], D))
        if kind == "retention":
            mat(a["ret_w_in"][0], D, 2 * D + H_R * DV_R)
            for h in range(H_R):
                for direction in range(2):
                    mat(a["ret_w_in"][0], D, DV_R, 2 * D + (1 + direction) * H_R * DV_R + h * DV_R)
            plan.extend(rows_of(a["ret_w_out"][0], H_R * DV_R))
        if kind == "mix":
            mat(a["w_mem_kv_2"][i], D, D)
            for part in ("cq", "ckv", "dq", "dk", "dv"):
                mat(a["w_in_2"][i], D, IN_SIZES[part], IN_AT[part])
            mat(a["w_mla_qb_2"][i], MLA_QL, MLA_H * MLA_QK)
            mat(a["w_mla_kvb_2"][i], MLA_KVL, MLA_H * (MLA_NOPE + MLA_V))
            for part in ("xq", "gate"):
                mat(a["w_in_2"][i], D, IN_SIZES[part], IN_AT[part])
            mat(a["w_mla_o_2"][i], MLA_H * MLA_V, D)
            mat(a["w_cross_o_2"][i], CROSS_H * CROSS_D, D)
            mat(a["w_diff_o_2"][i], D, D)
            mat(a["w_out_2"][i], D, D)
        if kind == "mlp":
            mat(a["w_mlp1_2"][i], D, D_MLP)
            mat(a["w_mlp2_2"][i], D_MLP, D)
    return plan


def gain_plan(a, stages):
    plan = []
    for kind, i, j in stages:
        if kind == "ffn":
            plan += [a["norm_gains"][i, 4 * j], a["norm_gains"][i, 4 * j + 1]]
        if kind in ("dilated", "retention"):
            plan += [a["norm_gains"][i, 2], a["norm_gains"][i, 3]]
        if kind == "mix":
            plan += [a["mem_gain_2"][i], a["g_mix_2"][i]]
            plan += [a["b_gate_2"][i, c * D:(c + 1) * D] for c in range(3)]
        if kind == "mlp":
            plan += [a["g_mlp_2"][i]]
    return plan


class WeightStream:
    RAW, SPLIT = 4, 4

    def __init__(self, nc, k, plan):
        self.k, self.plan, self.at, self.loaded, self.ready = k, plan, 0, {}, {}
        self.raw = [DmaSlot(nc, f"w{i}", k.sbuf(f"w_raw{i}", [P, TILE])) for i in range(self.RAW)]
        self.raw_free = [None] * self.RAW
        self.hi = [k.sbuf(f"w_hi{i}", [P, TILE], F32R) for i in range(self.SPLIT)]
        self.lo = [k.sbuf(f"w_lo{i}", [P, TILE], F32R) for i in range(self.SPLIT)]
        self.split_free = [None] * self.SPLIT
        self.hold_at = self.held = None
        self.share = 0

    def start(self):
        for i in range(min(self.RAW, len(self.plan))):
            self.load(i)

    def start_splits(self):
        for i in range(min(self.SPLIT, len(self.plan))):
            self.split(i)

    def load(self, i):
        view, nk, n = self.plan[i]
        slot = i % self.RAW
        self.k.sync.wait(self.raw_free[slot])
        dst = self.raw[slot].tensor[:, 0:nk * n].rearrange("p (k n) -> p k n", k=nk)
        self.loaded[i] = self.raw[slot].filled(self.k.sync.e.dma_start(dst, view))

    def split(self, i):
        _, nk, n = self.plan[i]
        act, dve = self.k.act, self.k.dve
        r, s, m = i % self.RAW, i % self.SPLIT, nk * n
        raw, hi, lo = self.raw[r].tensor[:, 0:m], self.hi[s][:, 0:m], self.lo[s][:, 0:m]
        act.wait(self.loaded.pop(i), self.split_free[s])
        t = act.do(act.e.activation(hi, raw, ACT.Copy))
        e = self.k.pool if self.share and i % self.share == 0 else dve
        e.wait(t)
        self.ready[i] = self.raw_free[r] = e.do(e.e.tensor_tensor(lo, raw, hi.bitcast(F32), ALU.subtract))
        if i + self.RAW < len(self.plan):
            self.load(i + self.RAW)

    def next(self, nk, n):
        i = self.at
        self.at += 1
        assert self.plan[i][1:] == (nk, n), (i, self.plan[i][1:], nk, n)
        return i, self.hi[i % self.SPLIT], self.lo[i % self.SPLIT], self.ready.pop(i)

    def hold_last(self, tiles):
        self.hold_at = self.at + tiles - 1

    def release(self):
        if self.held is not None:
            self.split(self.held)
        self.held = None

    def give(self, i, ticket):
        self.split_free[i % self.SPLIT] = ticket
        if i + self.SPLIT < len(self.plan):
            if i == self.hold_at:
                self.held = i + self.SPLIT
            else:
                self.split(i + self.SPLIT)


class GainStream:
    SLOTS = 2

    def __init__(self, nc, k, plan):
        self.k, self.plan, self.at, self.loaded = k, plan, 0, {}
        self.slot = [DmaSlot(nc, f"gain{i}", k.sbuf(f"gain{i}", [P, D])) for i in range(self.SLOTS)]

    def start(self):
        for i in range(min(self.SLOTS, len(self.plan))):
            self.load(i)

    def load(self, i):
        s = self.slot[i % self.SLOTS]
        self.loaded[i] = s.filled(self.k.pool.e.dma_start(s.tensor[:, :], self.plan[i].partition_broadcast(P)))

    def next(self):
        i = self.at
        self.at += 1
        return i, self.slot[i % self.SLOTS].tensor, self.loaded.pop(i)

    def give(self, i, *readers):
        if i + self.SLOTS < len(self.plan):
            self.k.pool.wait(*readers)
            self.load(i + self.SLOTS)


IDLE = "idle"


def together(*gens):
    gens = deque(gens)
    while gens:
        for _ in range(len(gens)):
            g = gens.popleft()
            try:
                state = next(g)
            except StopIteration:
                state = None
            else:
                gens.append(g)
            if state is not IDLE:
                break
        yield


class Kernel:
    def __init__(self, nc, a, stages):
        self.nc, self.a = nc, a
        self.pe, self.act, self.dve, self.pool = (
            Engine(nc, e, n) for e, n in ((nc.tensor, "pe"), (nc.scalar, "act"), (nc.vector, "dve"), (nc.gpsimd, "pool")))
        self.sync = Engine(nc, nc.sync, "sync")
        self.top = nc.sbuf_base
        psum = nc.alloc_psum_tensor("banks", [P, 8, BLOCK], F32)
        self.banks = Slots([psum[:, b, :] for b in range(8)])
        self.weights = WeightStream(nc, self, weight_plan(a, stages))
        self.gains = GainStream(nc, self, gain_plan(a, stages))
        self.x = self.sbuf("x", [P, HALVES, D])
        self.x_ready = [None] * HALVES
        self.tok = self.sbuf("tok", [P, HALVES, D])
        self.tok_free = [None, None]
        self.pending = None
        self.row_scale = self.sbuf("row_scale", [P, HALVES])
        at = self.room(2 * DC * SEQ * 4)
        self.xt = Transposed(nc, "xt", DC, at, at + DC * SEQ * 4)
        self.tmp = Slots([self.sbuf(f"tmp{i}", [P, BLOCK]) for i in range(4)])
        self.probs = Slots([self.sbuf(f"probs{i}", [P, HALVES * SEQ]) for i in range(3)])
        self.probs_t = Slots([self.sbuf(f"probs_t{i}", [P, 2, 2, P]) for i in range(2)])
        self.junk = self.sbuf("junk", [P, BLOCK], mybir.dt.bfloat16)
        self.junk_written = None
        self.stats = [self.sbuf(f"stat{i}", [P, 16]) for i in range(24)]
        self.stat_at = 0
        self.norm_sums, self.norm_at = [self.sbuf(f"norm_sums{i}", [P, 16]) for i in range(8)], 0
        self.minus_half = self.sbuf("minus_half", [P, 16])
        self.ident = self.sbuf("ident", [P, P])
        self.flip_tokens = self.sbuf("flip", [P, P])
        self.causal = self.sbuf("causal", [P, REL_W])
        self.small = self.sbuf("small", [P, sum(SMALL.values())])
        self.small_dma = DmaSlot(nc, "small", None)
        self.lam_products = self.sbuf("lam_products", [P, 2 * DIFF_D])
        self.rope = self.sbuf("rope", [P, 2, HALVES, (DIFF_D + MLA_ROPE) // 2])
        self.const_dma = DmaSlot(nc, "const", None)
        self.big = self.room(0)
        self.big_bytes = nc.sbuf_usable_end - self.big
        self.flip, self.act_share = 0, 2
        self.following, self.memory = None, None
        self.setup(stages)
        if stages[0][0] == "mix":
            self.weights.start_splits()
            self.drive(self.angles())
            self.following = stages[0]
            for _ in self.prelude():
                pass

    def room(self, size):
        at = (self.top + 31) // 32 * 32
        self.top = at + size
        assert self.top <= self.nc.sbuf_usable_end
        return at

    def sbuf(self, name, shape, dtype=F32):
        return self.nc.alloc_sbuf_tensor_at(name, shape, dtype, offset=self.room(int(np.prod(shape[1:])) * (2 if dtype == mybir.dt.bfloat16 else 4)))

    def place(self, name, kib, shape, dtype=F32):
        size = int(np.prod(shape[1:])) * 4
        assert kib * 1024 + size <= self.big_bytes, (name, kib, size, self.big_bytes)
        return self.nc.alloc_sbuf_tensor_at(name, shape, dtype, offset=self.big + int(kib * 1024))

    def place_t(self, name, kib, chunks):
        at, size = self.big + int(kib * 1024), chunks * SEQ * 4
        assert kib * 1024 + 2 * size <= self.big_bytes, (name, kib)
        return Transposed(self.nc, name, chunks, at, at + size)

    def stat(self, n):
        self.stat_at += 1
        return self.stats[self.stat_at % len(self.stats)][:, 0:n]

    def setup(self, stages):
        nc, a = self.nc, self.a
        c = self.const_dma
        act = self.act
        ident_in = c.filled(act.e.dma_start(self.ident[:, :], a["c_ident"]))
        xs = a["x"][0].rearrange("(h p) d -> h p d", p=P)
        for half in range(HALVES):
            dma = DmaSlot(nc, f"x{half}", None)
            self.x_ready[half] = dma.filled(act.e.dma_start(self.x[:, half, :], xs[half]))
        self.pe.wait(ident_in)
        self.half_set = self.dve.do(self.dve.e.memset(self.minus_half[:, :], -0.5))
        self.gains.start()
        self.weights.start()
        rest = DmaSlot(nc, "masks", None)
        for dst, src in ((self.flip_tokens, a["c_flip"]), (self.causal, a["c_causal"])):
            t = rest.filled(self.pool.e.dma_start(dst[:, :], src))
        self.masks_ready = t
        self.need_angles = any(kind == "mix" for kind, _, _ in stages)

    def turn_part(self, src, dst, half, some, ready, dst_free, order=None):
        pe, act, dve = self.pe, self.act, self.dve
        bank, free = self.banks.take()
        pe.wait(ready, free)
        for j, (c, s) in enumerate(some):
            last = pe.e.transpose(bank[:, j * P:(j + 1) * P], src(half, s), (order or self.ident)[:, :])
        t = pe.do(last)
        n = len(some)
        hi, lo = (x[:, half, some[0][0]:some[0][0] + n, :] for x in (dst.hi, dst.lo))
        view = bank[:, 0:n * P].rearrange("p (c t) -> p c t", c=n)
        act.wait(t, dst_free)
        h = act.do(act.e.activation(hi, view, ACT.Copy))
        dve.wait(h)
        v = dve.do(dve.e.tensor_tensor(lo, view, hi.bitcast(F32), ALU.subtract))
        self.banks.give(bank, v)
        for c, _ in some:
            dst.ready[half, c] = v

    def turn(self, src, dst, chunks, ready, dst_free, order=None):
        for half in range(HALVES):
            for c0 in range(0, len(chunks), 4):
                self.turn_part(src, dst, half, chunks[c0:c0 + 4], ready[half], dst_free, order)

    def turn_all(self, src, dst, n, ready, first=0, order=None):
        self.turn(lambda half, s: src(half)[:, s * P:(s + 1) * P], dst, [(first + c, c) for c in range(n)], ready,
                  dst.free, order)

    def block(self, xt, rows, n, first=0):
        pe = self.pe
        chunks, per = rows // P, TILE // n
        out = [self.banks.take() for _ in range(HALVES)]
        pe.wait(out[0][1], out[1][1])
        tickets = [None] * HALVES
        for k0 in range(0, chunks, per):
            nk = min(per, chunks - k0)
            i, hi, lo, ready = self.weights.next(nk, n)
            pe.wait(ready)
            for half in range(HALVES):
                bank = out[half][0][:, 0:n]
                for j in range(nk):
                    k = k0 + j
                    pe.wait(xt.ready[half, first + k])
                    ah, al = xt.hi[:, half, first + k, :], xt.lo[:, half, first + k, :]
                    wh, wl = hi[:, j * n:(j + 1) * n], lo[:, j * n:(j + 1) * n]
                    pe.e.matmul(bank, ah, wh, start=(k == 0), stop=False)
                    pe.e.matmul(bank, ah, wl, start=False, stop=False)
                    last = pe.e.matmul(bank, al, wh, start=False, stop=(k == chunks - 1))
                if k0 + nk == chunks or half == HALVES - 1:
                    tickets[half] = pe.do(last)
            self.weights.give(i, tickets[HALVES - 1])
            yield
        xt.free = tickets[HALVES - 1]
        return [b for b, _ in out], tickets

    def block_by_chunk(self, xt, rows):
        pe = self.pe
        out = [[self.banks.take() for _ in range(HALVES)] for _ in range(2)]
        pe.wait(*[free for pair in out for _, free in pair])
        chunks = rows // P
        tickets = [[None] * HALVES for _ in range(2)]
        for k in range(chunks):
            while any((half, k) not in xt.ready for half in range(HALVES)):
                yield
            i, hi, lo, ready = self.weights.next(1, D)
            pe.wait(ready)
            for c in range(2):
                for half in range(HALVES):
                    pe.wait(xt.ready[half, k])
                    bank, cols = out[c][half][0], slice(c * BLOCK, (c + 1) * BLOCK)
                    ah, al = xt.at(half, k)
                    pe.e.matmul(bank, ah, hi[:, cols], start=(k == 0), stop=False)
                    pe.e.matmul(bank, ah, lo[:, cols], start=False, stop=False)
                    tickets[c][half] = pe.do(pe.e.matmul(bank, al, hi[:, cols], start=False, stop=(k == chunks - 1)))
            self.weights.give(i, tickets[1][1])
            yield
        xt.free = tickets[1][1]
        return [([b for b, _ in out[c]], tickets[c]) for c in range(2)]

    def evacuate(self, dst, bank, ticket, free=None, scale=None):
        self.flip = (self.flip + 1) % 4
        e = self.act if self.flip < self.act_share else self.dve
        e.wait(ticket, free)
        if e is self.act:
            made = e.e.activation(dst, bank, ACT.Copy) if scale is None else e.e.activation(dst, bank, ACT.Copy, scale=scale)
        else:
            made = e.e.tensor_copy(dst, bank) if scale is None else e.e.tensor_scalar(dst, bank, scale, None, ALU.mult)
        return e.do(made)

    def project(self, xt, rows, n, dst, free=None, first=0):
        ready = [[] for _ in range(HALVES)]
        for c0, m in column_blocks(n):
            banks, tickets = yield from self.block(xt, rows, m, first)
            for half in range(HALVES):
                scale, scaled = xt.scale[half]
                t = self.evacuate(dst[:, half, c0:c0 + m], banks[half][:, 0:m], [tickets[half], scaled], free, scale)
                self.banks.give(banks[half], t)
                ready[half].append(t)
        return ready

    def pause(self, tiles, polls=8):
        mark = self.weights.at + tiles
        for _ in range(polls):
            if self.weights.at >= mark:
                return
            yield IDLE

    @staticmethod
    def drive(main, side=None, every=1, finish=True, steps=1):
        n = 0
        while True:
            try:
                next(main)
            except StopIteration as stop:
                result = stop.value
                break
            n += 1
            if side is not None and n % every == 0:
                for _ in range(steps):
                    next(side, None)
        if side is not None and finish:
            for _ in side:
                pass
        return result

    def square_sum(self, src, out, ready):
        act = self.act
        act.wait(ready, self.junk_written)
        self.junk_written = act.do(act.e.activation(self.junk[:, 0:src.shape[-1]], src, ACT.Square, accum_out=out))
        return self.junk_written

    def rstd(self, total, count, ready, factor=1.0, keep=None):
        dve, pool = self.dve, self.pool
        n = total.shape[-1]
        mean, out = self.stat(n), self.stat(n) if keep is None else keep
        dve.wait(ready)
        t = dve.do(dve.e.tensor_scalar(mean, total, 1.0 / (count * factor ** 2), EPS / factor ** 2, ALU.mult, ALU.add))
        pool.wait(t, self.half_set)
        return out, pool.do(pool.e.tensor_tensor(out, mean, self.minus_half[:, 0:n], ALU.pow))

    def row_rstd(self, srcs, count, ready, factor=1.0, keep=None):
        sums = self.stat(len(srcs))
        ts = [self.square_sum(s, sums[:, i:i + 1], r) for i, (s, r) in enumerate(zip(srcs, ready))]
        dve = self.dve
        total = sums
        if len(srcs) > 1:
            total = self.stat(1)
            dve.wait(*ts)
            ts = [dve.do(dve.e.tensor_reduce(total, sums, AX.X, ALU.add))]
        return self.rstd(total, count, ts, factor, keep)

    def feed(self, between=None):
        act, dve, pool, tok = self.act, self.dve, self.pool, self.tok
        gi, gain, g_ready = self.gains.next()
        cols = [slice(c, c + BLOCK) for c in range(0, D, BLOCK)]
        ready = {}

        def part(half, c):
            if self.pending:
                self.pending(half, c)
            e = dve if c == 0 else pool
            e.wait(self.x_ready[half], g_ready, self.tok_free[half])
            ready[half, c] = e.do(e.e.tensor_tensor(tok[:, half, cols[c]], self.x[:, half, cols[c]], gain[:, cols[c]], ALU.mult))

        def turned(half, c):
            self.turn_part(lambda h, s: tok[:, h, s * P:(s + 1) * P], self.xt, half, [(4 * c + j, 4 * c + j) for j in range(4)],
                           ready[half, c], self.xt.free)

        part(0, 0), part(1, 0)
        if between:
            part(0, 1), part(1, 1)
            self.weights.release()
            between()
            turned(0, 0), turned(1, 0)
        else:
            turned(0, 0)
            part(0, 1)
            turned(1, 0)
            part(1, 1)
        turned(0, 1), turned(1, 1)
        self.weights.release()
        if self.weights.at == 0 and not self.weights.ready:
            self.weights.start_splits()
        self.pending = None
        self.gains.give(gi, *ready.values())
        self.tok_free = [self.pe.last()] * HALVES
        for half in range(HALVES):
            self.xt.scale[half] = self.row_rstd([self.x[:, half, c] for c in cols], D, [self.x_ready[half]] * 2, keep=self.row_scale[:, half:half + 1])

    def last_normed(self, xt, rows, factor, by_chunk=False):
        dve, tok = self.dve, self.tok
        gi, gain, g_ready = self.gains.next()
        sums = [self.stat(2) for _ in range(HALVES)]
        summed, scaled = [[], []], {}
        if by_chunk:
            self.weights.hold_last(rows // P)
            both = yield from self.block_by_chunk(xt, rows)
        for c, (c0, m) in enumerate(column_blocks(D)):
            if c == 1 and not by_chunk:
                self.weights.hold_last(rows * BLOCK // (P * TILE))
            banks, ts = both[c] if by_chunk else (yield from self.block(xt, rows, m))
            for half in range(HALVES):
                s = self.square_sum(banks[half], sums[half][:, c:c + 1], ts[half])
                summed[half].append(s)
                dve.wait(s, g_ready, self.tok_free[half])
                t = dve.do(dve.e.tensor_tensor(tok[:, half, c0:c0 + m], banks[half], gain[:, c0:c0 + m], ALU.mult))
                self.banks.give(banks[half], t)
                scaled[half, c] = t
        scale = []
        for half in range(HALVES):
            total = self.stat(1)
            dve.wait(*summed[half])
            t = dve.do(dve.e.tensor_reduce(total, sums[half], AX.X, ALU.add))
            scale.append(self.rstd(total, D, t, factor))
        self.gains.give(gi, scaled[HALVES - 1, 1])

        def update(half, c):
            r, t = scale[half]
            cols = slice(c * BLOCK, (c + 1) * BLOCK)
            dve.wait(t, scaled[half, c], self.x_ready[half])
            xs = self.x[:, half, cols]
            self.x_ready[half] = dve.do(dve.e.scalar_tensor_tensor(xs, tok[:, half, cols], r, xs, ALU.mult, ALU.add))
            self.tok_free[half] = self.x_ready[half]

        self.pending = update

    def last_plain(self, xt, rows):
        dve = self.dve
        out = []
        for c, m in column_blocks(D):
            if c:
                self.weights.hold_last(rows * BLOCK // (P * TILE))
            out.append((yield from self.block(xt, rows, m)))

        def update(half, c):
            banks, ts = out[c]
            xs = self.x[:, half, c * BLOCK:(c + 1) * BLOCK]
            dve.wait(ts[half], self.x_ready[half])
            self.x_ready[half] = dve.do(dve.e.tensor_tensor(xs, banks[half], xs, ALU.add))
            self.banks.give(banks[half], self.x_ready[half])

        self.pending = update

    def hidden(self, n_hidden, gated, ht):
        act, dve = self.act, self.dve
        waiting = None

        def turn_block(c0, m, h, tickets):
            chunks = [(c0 // P + j, j) for j in range(m // P)]
            self.turn(lambda half, s: h[half][:, s * P:(s + 1) * P], ht, chunks, tickets, None)
            for half in range(HALVES):
                self.tmp.give(h[half], self.pe.last())

        for c0, m in column_blocks(n_hidden):
            banks, ts = yield from self.block(self.xt, D, m)
            if gated:
                up, up_ts = yield from self.block(self.xt, D, m)
            if waiting:
                turn_block(*waiting)
            h_tiles, h_ts = [], []
            for half in range(HALVES):
                r, r_ready = self.xt.scale[half]
                h, free = self.tmp.take()
                hm = h[:, 0:m]
                act.wait(ts[half], r_ready, free)
                t = act.do(act.e.activation(hm, banks[half][:, 0:m], ACT.Silu if gated else ACT.Relu, scale=r))
                self.banks.give(banks[half], t)
                dve.wait(t)
                if gated:
                    dve.wait(up_ts[half], r_ready)
                    v = dve.do(dve.e.scalar_tensor_tensor(hm, up[half][:, 0:m], r, hm, ALU.mult, ALU.mult))
                    self.banks.give(up[half], v)
                else:
                    v = dve.do(dve.e.tensor_tensor(hm, hm, hm, ALU.mult))
                h_tiles.append(h)
                h_ts.append(v)
            waiting = (c0, m, h_tiles, h_ts)

        def rest():
            yield
            turn_block(*waiting)
            yield
            yield from self.prelude()
        return rest()

    def ffn(self, i, j):
        self.feed()
        ht = self.place_t(f"ffn_ht{i}{j}", 0, D_FF // P)
        rest = self.drive(self.hidden(D_FF, True, ht), self.angles() if self.need_angles else None)
        self.drive(self.last_normed(ht, D_FF, 0.5), rest)

    def mlp(self, i, j):
        self.feed()
        ht = self.place_t(f"mlp_ht{i}", 0, D_MLP // P)
        rest = self.drive(self.hidden(D_MLP, False, ht))
        self.drive(self.last_plain(ht, D_MLP), rest)

    def heads_t(self, src, dst, heads, ready, free=None, order=None):
        return self.drive(self.heads_t_steps(src, dst, heads, ready, free, order))

    def heads_t_steps(self, src, dst, heads, ready, free=None, order=None):
        pe = self.pe
        out = []
        for h0 in range(0, heads, 2):
            bank, bank_free = self.banks.take()
            pe.wait(bank_free, *ready)
            d = src(0, h0).shape[-1]
            n = min(2, heads - h0)
            for h in range(n):
                for half in range(HALVES):
                    at = h * SEQ + half * P
                    last = pe.e.transpose(bank[0:d, at:at + P], src(half, h0 + h), (order or self.ident)[:, :])
            t = pe.do(last)
            view = bank[0:d, 0:n * SEQ].rearrange("p (h t) -> p h t", h=n)
            if len(dst.shape) == 4:
                view = view.rearrange("p h (s t) -> p h s t", s=HALVES)
            t = self.evacuate(dst[0:d, h0:h0 + n, :], view, t, free)
            self.banks.give(bank, t)
            out.append(t)
            yield
        return out

    def attention(self, heads, per_bank, done):
        pe, act, dve = self.pe, self.act, self.dve
        exps, turned, out = {}, {}, None
        keys_of = lambda h: (SEQ, P if h["causal"] else SEQ)

        def scores(h):
            bank, free = self.banks.take()
            pe.wait(free, *h["ready"])
            keys = keys_of(h)
            for s in range(2):
                last = pe.e.matmul(bank[:, s * SEQ:s * SEQ + keys[s]], h["q"](1 - s), h["k"][:, 0:keys[s]], start=True, stop=True)
            t = pe.do(last)
            p, free = self.probs.take()
            view = bank.rearrange("p (s k) -> p s k", s=2)
            pv = p[:, :].rearrange("p (s k) -> p s k", s=2)
            ts = []
            if h["bias"] is not None:
                b = h["bias"]
                dve.wait(t, free, h["bias_ready"](), self.masks_ready)
                if h["causal"]:
                    n = sum(keys)
                    t = dve.do(dve.e.scalar_tensor_tensor(p[:, 0:n], bank[:, 0:n], h["scale"], b, ALU.mult, ALU.add))
                else:
                    pair = bass.AP(b.tensor, b.offset, [list(b.ap[0]), [P, 2], [1, SEQ]])
                    t = dve.do(dve.e.scalar_tensor_tensor(pv, view, h["scale"], pair, ALU.mult, ALU.add))
                self.banks.give(bank, t)
                h["bias_used"](t)
                dve.wait(t)
                if h["causal"]:
                    for s in range(2):
                        t = dve.do(dve.e.tensor_reduce(h["nmax"][:, s:s + 1], pv[:, s, 0:keys[s]], AX.X, ALU.max, negate=True))
                else:
                    t = dve.do(dve.e.tensor_reduce(h["nmax"], pv, AX.X, ALU.max, negate=True))
                act.wait(t)
                for s in range(2):
                    row = pv[:, s, 0:keys[s]]
                    ts.append(act.do(act.e.activation(row, row, ACT.Exp, bias=h["nmax"][:, s:s + 1], accum_out=h["den"][:, s:s + 1])))
            else:
                raw = self.stat(2)
                dve.wait(t)
                t = dve.do(dve.e.tensor_reduce(raw, view, AX.X, ALU.max, negate=True))
                dve.wait(t)
                t = dve.do(dve.e.tensor_scalar(h["nmax"], raw, h["scale"], None, ALU.mult))
                act.wait(t, free)
                for s in range(2):
                    ts.append(act.do(act.e.activation(pv[:, s, :], view[:, s, :], ACT.Exp, bias=h["nmax"][:, s:s + 1],
                                                      scale=h["scale"], accum_out=h["den"][:, s:s + 1])))
                self.banks.give(bank, ts[-1])
            return p, ts[-1]

        def turn_probs(h, p, t):
            bank, free = self.banks.take()
            pe.wait(free, t)
            blocks = [(kh, s) for kh in range(2) for s in range(2) if kh * P < keys_of(h)[s]]
            for kh, s in blocks:
                last = pe.e.transpose(bank[:, (2 * kh + s) * P:(2 * kh + s + 1) * P],
                                      p[:, s * SEQ + kh * P:s * SEQ + (kh + 1) * P], self.ident[:, :])
            t = pe.do(last)
            self.probs.give(p, t)
            pt, free = self.probs_t.take()
            n = len(blocks) * P
            t = self.evacuate(pt[:, :, :, :].rearrange("p k s t -> p (k s t)")[:, 0:n], bank[:, 0:n], t, free)
            self.banks.give(bank, t)
            return pt, t

        def values(n, h, pt, t):
            nonlocal out
            j, dv = n % per_bank, h["dv"]
            if j == 0:
                out, free = self.banks.take()
                pe.wait(free)
            pe.wait(t)
            for s in range(2):
                at = (s * per_bank + j) * dv
                n_keys = keys_of(h)[s] // P
                for kh in range(n_keys):
                    last = pe.e.matmul(out[:, at:at + dv], pt[:, kh, s, :], h["v"](kh), start=(kh == 0), stop=(kh == n_keys - 1))
            t = pe.do(last)
            self.probs_t.give(pt, t)
            if j == per_bank - 1:
                done(out, n - j, t)

        n = len(heads)
        for i in range(n + 2):
            if i < n:
                exps[i] = scores(heads[i])
            if 0 <= i - 1 < n:
                turned[i - 1] = turn_probs(heads[i - 1], *exps.pop(i - 1))
            if i >= 2:
                values(i - 2, heads[i - 2], *turned.pop(i - 2))
            yield

    def bias_tables(self):
        nc, a, pe, act = self.nc, self.a, self.pe, self.act
        table = nc.dram_tensor("bias_by_distance", [len(GROUPS) * H_A, 2 * SEQ], F32, kind="Internal").ap()
        onehot = self.place("onehot", 16, [N_BUCKETS + 1, len(GROUPS), 2 * SEQ])
        rel = self.place("rel_bias_t", 22, [N_BUCKETS + 1, len(GROUPS) * H_A])
        rows = self.place("bias_rows", 24, [H_A, len(GROUPS), 2 * SEQ])
        dma = DmaSlot(nc, "bias_in", None)
        pool = self.pool
        pool.wait(self.x_ready)
        self.dve.wait(self.x_ready)
        one = self.dve.do(self.dve.e.memset(rel[N_BUCKETS:N_BUCKETS + 1, :], 1.0))
        dma.filled(pool.e.dma_start(onehot[:, :, :], a["c_onehot"]))
        t = dma.filled(pool.e.dma_start(rel[0:N_BUCKETS, :], a["rel_bias"].rearrange("h b -> b h"), allow_slow_non_contiguous=True))
        for _ in range(4):
            yield
        stored = DmaSlot(nc, "bias_out", None)
        copies = []
        for g in range(len(GROUPS)):
            bank, free = self.banks.take()
            pe.wait(free, t, one)
            m = pe.do(pe.e.matmul(bank[0:H_A, :], rel[:, g * H_A:(g + 1) * H_A], onehot[:, g, :], start=True, stop=True))
            act.wait(m)
            c = act.do(act.e.activation(rows[:, g, :], bank[0:H_A, :], ACT.Copy))
            self.banks.give(bank, c)
            copies.append(c)
        pool.wait(copies)
        t = stored.filled(pool.e.dma_start(table.rearrange("(g h) r -> h g r", g=len(GROUPS)), rows[:, :, :]))
        return table, t

    def dilated(self, i, j):
        nc, dve, act, pool = self.nc, self.dve, self.act, self.pool
        self.feed()
        self.pe.wait(self.masks_ready)
        q = self.place("da_q", 0, [P, HALVES, D])
        k = self.place("da_k", 8, [P, HALVES, D])
        qt = self.place("da_qt", 16, [P, DC, SEQ])
        kt = self.place("da_kt", 24, [P, DC, SEQ])
        vs = [self.place(f"da_v{n}", 32 + 8 * n, [P, HALVES, D]) for n in range(2)]
        outs = [self.tok] + [self.place(f"da_o{n}", 48 + 8 * n, [P, HALVES, D]) for n in range(2)]
        bias = [DmaSlot(nc, f"bias{n}", self.place(f"da_bias{n}", 64 + 1.5 * n, [P, REL_W])) for n in range(6)]
        heads_n = len(GROUPS) * H_A
        nmax = self.place("da_nmax", 73, [P, heads_n, 2])
        den = self.place("da_den", 73.5, [P, heads_n, 2])
        bias_loaded, bias_used = {}, {}
        table = table_ready = None

        def load_bias(n):
            s = bias[n % len(bias)]
            src = bass.AP(table.tensor, n * 2 * SEQ, [[1, P], [1, REL_W]])
            pool.wait(table_ready, bias_used.get(n - len(bias)), self.x_ready)
            bias_loaded[n] = s.filled(pool.e.dma_start(s.tensor[:, :], src))

        def biases():
            nonlocal table, table_ready
            table, table_ready = yield from self.bias_tables()
            for n in range(len(bias)):
                load_bias(n)

        def used(n):
            def note(t):
                bias_used[n] = t
                if n + len(bias) < heads_n:
                    load_bias(n + len(bias))
            return note

        side, qk_free, over = biases(), None, [None] * (len(GROUPS) + 2)

        kept = []
        low, coef, part = (self.place(f"da_{n}", 74 + 0.5 * m, [P, 3, H_A, 2]) for m, n in enumerate(("low", "coef", "part")))

        def combine(bank, h0, t):
            self.xt.ready.update(held)
            held.clear()
            at = slice(h0, h0 + 4)
            by_group = lambda z: z[:, :, :].rearrange("p (g h) s -> p g h s", g=3)
            nm, dn = by_group(nmax), by_group(den)
            dve.wait(t, act.last(), kept)
            u = dve.do(dve.e.tensor_tensor(low[:, 0, at, :], nm[:, 0, at, :], nm[:, 1, at, :], ALU.min))
            dve.wait(u)
            u = dve.do(dve.e.tensor_tensor(low[:, 0, at, :], low[:, 0, at, :], nm[:, 2, at, :], ALU.min))
            dve.wait(u)
            for g in range(3):
                u = dve.do(dve.e.tensor_tensor(coef[:, g, at, :], low[:, 0, at, :], nm[:, g, at, :], ALU.subtract))
            act.wait(u)
            u = act.do(act.e.activation(coef[:, :, at, :], coef[:, :, at, :], ACT.Exp))
            dve.wait(u)
            u = dve.do(dve.e.tensor_tensor(part[:, :, at, :], coef[:, :, at, :], dn[:, :, at, :], ALU.mult))
            for g in range(1, 3):
                dve.wait(u)
                u = dve.do(dve.e.tensor_tensor(part[:, 0, at, :], part[:, 0, at, :], part[:, g, at, :], ALU.add))
            dve.wait(u)
            u = dve.do(dve.e.reciprocal(part[:, 0, at, :], part[:, 0, at, :]))
            dve.wait(u)
            for g in range(3):
                u = dve.do(dve.e.tensor_tensor(coef[:, g, at, :], coef[:, g, at, :], part[:, 0, at, :], ALU.mult))
            yield
            coefs = u
            cols = slice(h0 * DH_A, (h0 + 4) * DH_A)
            shaped = lambda z: z.rearrange("p (h d) -> p h d", d=DH_A)
            ready = []
            for s in range(2):
                c = [coef[:, g, at, s:s + 1].to_broadcast([P, 4, DH_A]) for g in range(3)]
                o = [z[:, s, cols] for z in outs]
                pool.wait(coefs)
                pool.do(pool.e.tensor_tensor(shaped(o[0]), shaped(o[0]), c[0], ALU.mult))
                w = pool.do(pool.e.tensor_tensor(shaped(o[1]), shaped(o[1]), c[1], ALU.mult))
                dve.wait(coefs)
                u = dve.do(dve.e.tensor_tensor(shaped(o[2]), shaped(bank[:, s * 4 * DH_A:(s + 1) * 4 * DH_A]), c[2], ALU.mult))
                dve.wait(u)
                dve.wait(w)
                u = dve.do(dve.e.tensor_tensor(o[0], o[0], o[1], ALU.add))
                dve.wait(u)
                ready.append(dve.do(dve.e.tensor_tensor(o[0], o[0], o[2], ALU.add)))
                yield
            self.banks.give(bank, ready[-1])
            c0 = h0 * DH_A // P
            for half in range(HALVES):
                self.turn_part(lambda h, c: self.tok[:, 1 - h, c * P:(c + 1) * P], self.xt, half, [(c0, c0), (c0 + 1, c0 + 1)],
                               ready[1 - half], self.xt.free, order=self.flip_tokens)
                if h0 + 4 < H_A:
                    held.update({(half, c): self.xt.ready.pop((half, c)) for c in (c0, c0 + 1)})
            self.tok_free = [self.pe.last()] * HALVES

        held = {}
        combining = deque()

        def last_group(attention):
            for _ in attention:
                if combining and next(combining[0], IDLE) is IDLE:
                    combining.popleft()
                yield
            for c in combining:
                for _ in c:
                    yield

        def qkv(g):
            ready = []
            for dst, free in ((q, qk_free), (k, qk_free), (vs[g % 2], over[g])):
                ready.append((yield from self.project(self.xt, D, D, dst, free)))
            return ready

        for g in range(len(GROUPS)):
            v = vs[g % 2]
            q_ready, k_ready, v_ready = self.drive(qkv(g), side, 2)
            side_done = over[g + 1] = self.pe.last()
            qts = self.heads_t(lambda half, c: q[:, half, c * P:(c + 1) * P], qt, DC, q_ready, [side_done, table_ready], self.flip_tokens)
            kts = self.heads_t(lambda half, c: k[:, half, c * P:(c + 1) * P], kt, DC, k_ready, [side_done, table_ready])
            qk_free = self.pe.last()
            heads = []
            for h in range(H_A):
                n, at = g * H_A + h, DH_A * (h % 2)
                heads.append(dict(
                    q=lambda half, c=h // 2, at=at: qt[at:at + DH_A, c, half * P:(half + 1) * P],
                    k=kt[at:at + DH_A, h // 2, :],
                    v=lambda kh, v=v, h=h: v[:, kh, h * DH_A:(h + 1) * DH_A],
                    dv=DH_A, scale=DH_A ** -0.5, causal=False, bias=bias[n % len(bias)].tensor[:, :],
                    bias_ready=lambda n=n: bias_loaded[n], bias_used=used(n),
                    nmax=nmax[:, n, :], den=den[:, n, :], ready=[qts[h // 4], kts[h // 4]] + v_ready))
            o = outs[g]

            def keep(bank, h0, t, o=o):
                view = bank.rearrange("p (s c) -> p s c", s=2)
                t = self.evacuate(o[:, :, h0 * DH_A:(h0 + 4) * DH_A], view, t, self.tok_free)
                self.banks.give(bank, t)
                kept.append(t)

            side = self.attention(heads, 4, keep if g < len(GROUPS) - 1 else lambda *args: combining.append(combine(*args)))
        self.xt.ready = {}
        self.drive(self.last_normed(self.xt, D, 1.0, by_chunk=True), last_group(side))

    def rotate(self, first, second, cos, sin, ready):
        dve, pool = self.dve, self.pool
        dims = [int(v) for v in first.shape[1:]]
        size = int(np.prod(dims))
        tiles = [self.tmp.take() for _ in range(3)]
        a, b, c = (self.shaped(t[:, 0:size], dims) for t, _ in tiles)
        dve.wait(ready, *[f for _, f in tiles])
        pool.wait(ready, *[f for _, f in tiles])
        pool.do(pool.e.tensor_tensor(c, first, sin, ALU.mult))
        w = dve.do(dve.e.tensor_tensor(b, second, sin, ALU.mult))
        t = dve.do(dve.e.tensor_tensor(a, first, cos, ALU.mult))
        pool.wait(w)
        u = pool.do(pool.e.tensor_tensor(second, second, cos, ALU.mult))
        dve.wait(t, u)
        dve.do(dve.e.tensor_tensor(first, a, b, ALU.subtract))
        u = dve.do(dve.e.tensor_tensor(second, second, c, ALU.add))
        for t_, _ in tiles:
            self.tmp.give(t_, u)
        return u

    @staticmethod
    def shaped(ap, dims):
        if len(dims) == 1:
            return ap
        return ap.rearrange("p (a b) -> p a b", a=dims[0])

    def decays(self, rel_dist):
        nc, a, act, dve, pool = self.nc, self.a, self.act, self.dve, self.pool
        n = 2 * H_R
        w = self.place("ret_small", 66, [P, 12, n])
        dma = DmaSlot(nc, "decay", None)
        pool.wait(self.x_ready)
        dma.filled(pool.e.dma_start(rel_dist[:, :], a["c_dist"]))
        t = dma.filled(pool.e.dma_start(w[:, 0, :], a["ret_decay_logit"][0].rearrange("a h -> (a h)").partition_broadcast(P)))
        col = lambda i: w[:, i, :]

        def step(fn, out, *args):
            nonlocal t
            dve.wait(t)
            t = dve.do(fn(col(out), *args))

        yield
        act.wait(t)
        t = act.do(act.e.activation(col(1), col(0), ACT.Exp))
        step(dve.e.tensor_scalar, 2, col(1), -1.0, 2.0, ALU.mult, ALU.add)
        step(dve.e.reciprocal, 2, col(2))
        step(dve.e.tensor_tensor, 2, col(2), col(1), ALU.mult)
        step(dve.e.tensor_tensor, 3, col(2), col(2), ALU.mult)
        step(dve.e.tensor_scalar, 4, col(3), 1.0 / 13, 1.0 / 11, ALU.mult, ALU.add)
        for m in (9, 7, 5, 3, 1):
            step(dve.e.tensor_tensor, 4, col(4), col(3), ALU.mult)
            step(dve.e.tensor_scalar, 4, col(4), 1.0 / m, None, ALU.add)
            yield
        step(dve.e.tensor_tensor, 4, col(4), col(2), ALU.mult)
        step(dve.e.tensor_scalar, 4, col(4), -2.0, None, ALU.mult)
        step(dve.e.tensor_scalar, 5, col(1), -1.0, 1.0, ALU.mult, ALU.add)
        act.wait(t)
        t = act.do(act.e.activation(col(6), col(5), ACT.Ln))
        step(dve.e.tensor_scalar, 7, col(1), 0.25, None, ALU.is_lt)
        step(dve.e.tensor_scalar, 8, col(7), -1.0, 1.0, ALU.mult, ALU.add)
        step(dve.e.tensor_tensor, 4, col(4), col(7), ALU.mult)
        step(dve.e.tensor_tensor, 6, col(6), col(8), ALU.mult)
        step(dve.e.tensor_tensor, 9, col(6), col(4), ALU.add)
        tiles = []
        for direction in range(2):
            span, free = self.tmp.take()
            dve.wait(t, free)
            sign = 1.0 if direction == 0 else -1.0
            s = dve.do(dve.e.tensor_scalar(span[:, 0:REL_W], rel_dist[:, :], sign, 0.0, ALU.mult, ALU.max))
            for h in range(H_R):
                out = self.place(f"decay{direction}{h}", 68 + 1.5 * (direction * H_R + h), [P, REL_W])
                lg = w[:, 9, direction * H_R + h:direction * H_R + h + 1]
                act.wait(s, t)
                e = act.do(act.e.activation(out[:, :], span[:, 0:REL_W], ACT.Exp, scale=lg))
                dve.wait(e)
                t = dve.do(dve.e.scalar_tensor_tensor(out[:, :], rel_dist[:, :], 0.0, out[:, :],
                                                      ALU.is_ge if direction == 0 else ALU.is_le, ALU.mult))
                tiles.append(out)
                yield
            self.tmp.give(span, e)
        return tiles, t

    def retention(self, i, j):
        nc, pe, act, dve, pool = self.nc, self.pe, self.act, self.dve, self.pool
        q = self.place("re_q", 0, [P, HALVES, D])
        k = self.place("re_k", 8, [P, HALVES, D])
        qt = self.place("re_qt", 16, [P, DC, SEQ])
        kt = self.place("re_kt", 24, [P, DC, SEQ])
        v = self.place("re_v", 32, [P, HALVES, H_R * DV_R])
        pair_at = (48, 56, 0, 8)
        gates = [[self.place(f"re_g{h}{d}", pair_at[h] + 4 * d, [P, HALVES, DV_R]) for d in range(2)] for h in range(H_R)]
        yt_at = (80,) + pair_at[:3]
        yt = Joined([self.place_t(f"re_yt{h}", yt_at[h], DV_R // P) for h in range(H_R)], DV_R // P)
        dist = self.place("re_dist", 64, [P, REL_W])
        rope = self.place("re_rope", 84, [P, 2, HALVES, DK_R // 2])
        dma = DmaSlot(nc, "ret_rope", None)
        self.feed()
        pool.wait(self.x_ready)
        rope_ready = dma.filled(pool.e.dma_start(rope[:, :, :, :], self.a["c_ret_rope"]))
        got = {}

        def qkv():
            got["q"] = yield from self.project(self.xt, D, D, q)
            got["k"] = yield from self.project(self.xt, D, D, k)
            got["v"] = yield from self.project(self.xt, D, H_R * DV_R, v)

        def rotations():
            got["decay"] = yield from self.decays(dist)
            for name, z, zt, factor in (("q", q, qt, 1.0), ("k", k, kt, DK_R ** -0.5)):
                while name not in got:
                    yield
                rot = []
                for half in range(HALVES):
                    heads = z[:, half, :].rearrange("p (h two d) -> p h two d", h=H_R, two=2)
                    cos, sin = (rope[:, m, half:half + 1, :].to_broadcast([P, H_R, DK_R // 2]) for m in range(2))
                    t = self.rotate(heads[:, :, 0, :], heads[:, :, 1, :], cos, sin, got[name][half] + [rope_ready])
                    yield
                    if factor != 1.0:
                        act.wait(t)
                        t = act.do(act.e.activation(z[:, half, :], z[:, half, :], ACT.Copy, scale=factor))
                        yield
                    rot.append(t)
                yield
                yield
                got[name + "t"] = self.heads_t(lambda half, c, z=z: z[:, half, c * P:(c + 1) * P], zt, DC, rot)
                yield

        self.drive(qkv(), rotations())
        rope_used = dve.last()
        v_ready, (decay, decay_ready) = got["v"], got["decay"]

        def gate_blocks():
            for h in range(H_R):
                for direction in range(2):
                    banks, ts = yield from self.block(self.xt, D, DV_R)
                    for half in range(HALVES):
                        r, r_ready = self.xt.scale[half]
                        act.wait(ts[half], r_ready)
                        t = act.do(act.e.activation(gates[h][direction][:, half, :], banks[half], ACT.Silu, scale=r))
                        self.banks.give(banks[half], t)
                        got["gate", h, direction, half] = t

        per = DK_R // P

        def heads():
            to_turn = None
            for h in range(H_R):
                weighted = []
                for jh in range(HALVES):
                    bank, free = self.banks.take()
                    pe.wait(free, got["qt"], got["kt"])
                    for c in range(per):
                        last = pe.e.matmul(bank[:, 0:SEQ], kt[:, h * per + c, jh * P:(jh + 1) * P], qt[:, h * per + c, :],
                                           start=(c == 0), stop=(c == per - 1))
                    t = pe.do(last)
                    both, free = self.probs.take()
                    for direction in range(2):
                        dk = decay[direction * H_R + h][:, P * (1 - jh):P * (1 - jh) + SEQ]
                        dve.wait(t, free, decay_ready)
                        u = dve.do(dve.e.tensor_tensor(both[:, direction * SEQ:(direction + 1) * SEQ], bank[:, 0:SEQ], dk, ALU.mult))
                    self.banks.give(bank, u)
                    weighted.append((both, u))
                    yield
                if to_turn:
                    yield from turn_head(*to_turn)
                    if h < H_R - 1:
                        yt.note(h - 1)
                y_ready = []
                for half in range(HALVES):
                    for direction in range(2):
                        bank, free = self.banks.take()
                        keys = range(0, half + 1) if direction == 0 else range(half, HALVES)
                        pe.wait(free, [w[1] for w in weighted], v_ready)
                        for n, jh in enumerate(keys):
                            at = direction * SEQ + half * P
                            last = pe.e.matmul(bank, weighted[jh][0][:, at:at + P], v[:, jh, h * DV_R:(h + 1) * DV_R],
                                               start=(n == 0), stop=(n == len(keys) - 1))
                        t = pe.do(last)
                        st, mv, shift = self.stat(6), self.stat(2), self.stat(1)
                        dve.wait(t)
                        u = dve.do(dve.e.bn_stats(st, bank))
                        dve.wait(u)
                        u = dve.do(dve.e.bn_aggr(mv, st))
                        r, rt = self.rstd(mv[:, 1:2], 1.0, u)
                        dve.wait(rt)
                        u = dve.do(dve.e.scalar_tensor_tensor(shift, mv[:, 0:1], -1.0, r, ALU.mult, ALU.mult))
                        tmp, free = self.tmp.take()
                        act.wait(u, rt, free)
                        u = act.do(act.e.activation(tmp[:, :], bank, ACT.Identity, bias=shift, scale=r))
                        self.banks.give(bank, u)
                        yield
                        while ("gate", h, direction, half) not in got:
                            yield
                        g = gates[h][direction][:, half, :]
                        dve.wait(u, got["gate", h, direction, half])
                        u = dve.do(dve.e.tensor_tensor(g, g, tmp[:, :], ALU.mult))
                        self.tmp.give(tmp, u)
                    dve.wait(u)
                    g0, g1 = (gates[h][d][:, half, :] for d in range(2))
                    y_ready.append(dve.do(dve.e.tensor_tensor(g0, g0, g1, ALU.add)))
                for both, _ in weighted:
                    self.probs.give(both, pe.last())
                to_turn = h, y_ready
            yt.note(H_R - 2)
            for _ in range(3):
                yield
            yield from turn_head(*to_turn)
            yt.note(H_R - 1)

        def turn_head(h, y_ready):
            for half in range(HALVES):
                self.turn_part(lambda half, c: gates[h][0][:, half, c * P:(c + 1) * P], yt.parts[h], half,
                               [(c, c) for c in range(DV_R // P)], y_ready[half], [rope_used, pe.last(), dve.last()])
                yield

        side = heads()
        self.drive(gate_blocks(), side, 1, finish=False)
        self.drive(self.last_normed(yt, H_R * DV_R, 1.0, by_chunk=True), side)

    def angles(self):
        a, act, dve, pool, nc = self.a, self.act, self.dve, self.pool, self.nc
        nf = (DIFF_D + MLA_ROPE) // 2
        pos_i = nc.alloc_sbuf_tensor_at("pos_i", [P, HALVES, 1], I32, offset=self.big + 60 * 1024)
        pos = self.place("pos_f", 60.25, [P, HALVES, 1])
        freq = self.place("freq", 60.5, [P, nf])
        ang = self.place("ang", 61, [P, HALVES, nf])
        turns = self.place("turns", 61.5, [P, HALVES, nf])
        red = self.place("reduced", 62, [P, HALVES, nf])
        dma = DmaSlot(nc, "angles", None)
        pool.wait(self.x_ready)
        dma.filled(pool.e.dma_start(pos_i[:, :, :], a["positions_2"].rearrange("o (h p) -> p h o", p=P), allow_slow_non_contiguous=True))
        t = dma.filled(pool.e.dma_start(freq[:, :], a["c_inv_freq"][0].partition_broadcast(P)))
        for _ in range(8):
            yield
        dve.wait(t)
        t = dve.do(dve.e.tensor_copy(pos[:, :, :], pos_i[:, :, :]))
        dve.wait(t)
        for half in range(HALVES):
            t = dve.do(dve.e.tensor_scalar(ang[:, half, :], freq[:, :], pos[:, half, :], None, ALU.mult))
        magic = 1.5 * 2 ** 23
        two_pi = 2 * math.pi
        parts = []
        rest = two_pi
        for bits in (9, 9, 11):
            e = math.floor(math.log2(abs(rest)))
            step = 2.0 ** (e - bits + 1)
            parts.append(math.floor(rest / step) * step)
            rest -= parts[-1]
        parts.append(float(np.float32(rest)))
        for which, shift in ((0, 0.25), (1, 0.0)):
            dve.wait(t)
            t = dve.do(dve.e.tensor_scalar(turns[:, :, :], ang[:, :, :], 1.0 / two_pi, shift, ALU.mult, ALU.add))
            dve.wait(t)
            t = dve.do(dve.e.tensor_scalar(turns[:, :, :], turns[:, :, :], magic, None, ALU.add))
            dve.wait(t)
            t = dve.do(dve.e.tensor_scalar(turns[:, :, :], turns[:, :, :], -magic, None, ALU.add))
            src = ang
            for part in parts:
                dve.wait(t)
                yield
                t = dve.do(dve.e.scalar_tensor_tensor(red[:, :, :], turns[:, :, :], -part, src[:, :, :], ALU.mult, ALU.add))
                src = red
            dve.wait(t)
            t = dve.do(dve.e.tensor_scalar(red[:, :, :], red[:, :, :], shift * two_pi, math.pi, ALU.add, ALU.min))
            dve.wait(t)
            t = dve.do(dve.e.tensor_scalar(red[:, :, :], red[:, :, :], -math.pi, None, ALU.max))
            act.wait(t)
            t = act.do(act.e.activation(self.rope[:, which, :, :], red[:, :, :], ACT.Sin))
        self.rope_ready = t
        self.need_angles = False

    def head_norm(self, z, heads, d, gain, ready, factor=1.0):
        act, dve = self.act, self.dve
        sums = self.norm_sums[self.norm_at % len(self.norm_sums)][:, 0:heads]
        self.norm_at += 1
        per = max(1, BLOCK // d)
        if heads * d <= BLOCK:
            per = heads
        for h0 in range(0, heads, per):
            n = min(per, heads - h0)
            tmp, free = self.tmp.take()
            sq = tmp[:, 0:n * d].rearrange("p (h d) -> p h d", h=n)
            act.wait(ready, free)
            t = act.do(act.e.activation(sq, z[:, h0:h0 + n, :], ACT.Square))
            dve.wait(t)
            t = dve.do(dve.e.tensor_reduce(sums[:, h0:h0 + n], sq, AX.X, ALU.add))
            self.tmp.give(tmp, t)
            yield
        r, t = self.rstd(sums, d, t, factor)
        yield from self.pause(2)
        dve.wait(t, ready)
        rb = r.rearrange("p (h o) -> p h o", o=1).to_broadcast([P, heads, d])
        t = dve.do(dve.e.tensor_tensor(z, z, rb, ALU.mult))
        yield
        dve.wait(t, self.small_ready)
        gb = gain.rearrange("p (o d) -> p o d", o=1).to_broadcast([P, heads, d])
        return dve.do(dve.e.tensor_tensor(z, z, gb, ALU.mult))

    def wide_norm(self, z, d, gain, ready):
        r, t = self.row_rstd([z], d, [ready])
        self.dve.wait(t, self.small_ready)
        return self.dve.do(self.dve.e.scalar_tensor_tensor(z, z, r, gain, ALU.mult, ALU.mult))

    def prelude(self):
        if self.following is None or self.following[0] != "mix":
            return
        a, pe, act, dve, pool = self.a, self.pe, self.act, self.dve, self.pool
        layer = self.following[1]
        L = f"{layer}"
        pool.wait(self.x_ready, pe.last())
        mem = self.place("mx_mem" + L, 80, [P, HALVES, D])
        mem_t = self.place_t("mx_mem_t" + L, 64, DC)
        mem_dma = DmaSlot(self.nc, "mem" + L, None)
        m_ready = mem_dma.filled(pool.e.dma_start(mem[:, :, :], a["mem_2"][0].rearrange("(h p) d -> p h d", p=P)))
        for name, n in SMALL.items():
            at = SMALL_AT[name]
            src = a[name][layer]
            if name == "diff_lambda_2":
                src = src.rearrange("a b -> (a b)")
            t = self.small_dma.filled(pool.e.dma_start(self.small[:, at:at + n], src.partition_broadcast(P)))
        self.small_ready = t
        yield
        lam_init = 0.8 - 0.6 * math.exp(-0.3 * layer)
        lam = self.place("lam" + L, 88, [P, 8])
        lv = self.small_of("diff_lambda_2").rearrange("p (a two d) -> p a two d", a=2, two=2)
        prod = self.lam_products[:, :].rearrange("p (a d) -> p a d", a=2)
        dve.wait(t, self.x_ready)
        t = dve.do(dve.e.tensor_tensor(prod, lv[:, :, 0, :], lv[:, :, 1, :], ALU.mult))
        dve.wait(t)
        t = dve.do(dve.e.tensor_reduce(lam[:, 0:2], prod, AX.X, ALU.add))
        act.wait(t)
        t = act.do(act.e.activation(lam[:, 2:4], lam[:, 0:2], ACT.Exp))
        dve.wait(t)
        t = dve.do(dve.e.tensor_tensor(lam[:, 4:5], lam[:, 2:3], lam[:, 3:4], ALU.subtract))
        dve.wait(t)
        lam_ready = dve.do(dve.e.tensor_scalar(lam[:, 5:6], lam[:, 4:5], lam_init, None, ALU.add))
        yield
        gi, gain, g_ready = self.gains.next()
        ts = []
        for half in range(HALVES):
            r, t = self.row_rstd([mem[:, half, 0:BLOCK], mem[:, half, BLOCK:D]], D, [m_ready] * 2)
            yield
            dve.wait(t, g_ready)
            ts.append(dve.do(dve.e.scalar_tensor_tensor(mem[:, half, :], mem[:, half, :], r, gain[:, :], ALU.mult, ALU.mult)))
            yield
        self.gains.give(gi, *ts)
        for half in range(HALVES):
            for c0 in range(0, DC, 4):
                self.turn_part(lambda h, c: mem[:, h, c * P:(c + 1) * P], mem_t, half, [(c0 + c, c0 + c) for c in range(4)], ts[half], None)
                yield
        self.memory = mem_t, lam, lam_ready, pe.last()

    def small_of(self, name):
        return self.small[:, SMALL_AT[name]:SMALL_AT[name] + SMALL[name]]

    def mix(self, layer, _):
        nc, a, pe, act, dve, pool = self.nc, self.a, self.pe, self.act, self.dve, self.pool
        L = f"{layer}"
        small = self.small_of
        lam_init = 0.8 - 0.6 * math.exp(-0.3 * layer)
        mem_t, lam, lam_ready, mem_turned = self.memory

        q = self.place("mx_q" + L, 0, [P, HALVES, D])
        k = self.place("mx_k" + L, 8, [P, HALVES, D])
        low_t = self.place_t("mx_low_t" + L, 16, (MLA_QL + MLA_KVL) // P)
        mq = self.place("mx_mq" + L, 26, [P, HALVES, MLA_H * MLA_QK])
        xq = self.place("mx_xq" + L, 16, [P, HALVES, CROSS_H * CROSS_D])
        gates = [self.place(f"mx_gate{L}{n}", at, [P, HALVES, D])
                 for n, at in enumerate((8, 24, 16))]
        o_diff = self.place("mx_o_diff" + L, 0, [P, HALVES, D])
        v = self.place("mx_v" + L, 32, [P, HALVES, D])
        ck = self.place("mx_ck" + L, 26, [P, HALVES, CROSS_H * CROSS_D])
        qt = self.place("mx_qt" + L, 40, [P, DC, SEQ])
        kt = self.place("mx_kt" + L, 48, [P, DC, SEQ])
        diff_t = self.place_t("mx_diff_t" + L, 40, DC)
        kv = self.place("mx_kv" + L, 56, [P, HALVES, MLA_H * (MLA_NOPE + MLA_V)])
        mqt = self.place("mx_mqt" + L, 64, [P, MLA_H, SEQ])
        mkt = self.place("mx_mkt" + L, 72, [P, MLA_H, SEQ])
        mc_t = self.place_t("mx_mc_t" + L, 64, DC)
        ckt = self.place("mx_ckt" + L, 80, [P, CROSS_H, SEQ])
        cv = self.place("mx_cv" + L, 84, [P, HALVES, CROSS_H * CROSS_D])
        ckv_at = D - MLA_KVL - MLA_ROPE
        kr = ckv_at + MLA_KVL
        low = self.tok
        kcat = self.tok[:, :, 0:MLA_H * MLA_QK]
        o_mla, o_cross = self.tok[:, :, 0:MLA_H * MLA_V], self.tok[:, :, MLA_H * MLA_V:D]
        cqt = o_cross.rearrange("p s (h t) -> p h s t", h=CROSS_H)
        per_kv = MLA_NOPE + MLA_V
        n_heads = 2 * DIFF_H + MLA_H + CROSS_H
        nmax = self.place("mx_nmax" + L, 88.125, [P, n_heads, 2])
        den = self.place("mx_den" + L, 88.375, [P, n_heads, 2])
        rope = lambda which, half, lo, n, heads: self.rope[:, which, half:half + 1, lo:lo + n].to_broadcast([P, heads, n])
        got = {}

        def memory_kv():
            got["ck"] = self.drive(self.project(mem_t, D, D // 2, ck, pe.last()))
            got["cv"] = self.drive(self.project(mem_t, D, D // 2, cv, mem_turned))

        self.feed(memory_kv)

        def projections():
            got["cq"] = yield from self.project(self.xt, D, MLA_QL, low[:, :, 0:MLA_QL], self.tok_free)
            got["ckv"] = yield from self.project(self.xt, D, MLA_KVL + MLA_ROPE, low[:, :, ckv_at:D], self.tok_free)
            got["q"] = yield from self.project(self.xt, D, D, q)
            got["k"] = yield from self.project(self.xt, D, D, k)
            got["v"] = yield from self.project(self.xt, D, D, v)
            yield from need("low_t", "ckt")
            got["mq"] = yield from self.project(low_t, MLA_QL, MLA_H * MLA_QK, mq)
            got["kv"] = yield from self.project(low_t, MLA_KVL, MLA_H * per_kv, kv, first=MLA_QL // P)
            got["xq"] = yield from self.project(self.xt, D, CROSS_H * CROSS_D, xq, low_t.free)
            for g, needed in enumerate(("kt", "mqt", "cqt")):
                yield from need(needed)
                gi, b, b_ready = self.gains.next()
                ts_gate = [[], []]
                for c0, m in column_blocks(D):
                    banks, ts = yield from self.block(self.xt, D, m)
                    for half in range(HALVES):
                        r, r_ready = self.xt.scale[half]
                        dve.wait(ts[half], r_ready, b_ready)
                        t = dve.do(dve.e.scalar_tensor_tensor(gates[g][:, half, c0:c0 + m], banks[half], r, b[:, c0:c0 + m], ALU.mult, ALU.add))
                        self.banks.give(banks[half], t)
                self.gains.give(gi, t)
                got["gate", g] = t

        def turn_heads(name, *args):
            yield from self.pause(4)
            got[name] = yield from self.heads_t_steps(*args)

        def need(*names):
            while any(name not in got for name in names):
                yield IDLE

        def diff_part(name, z, half, gain):
            heads = z[:, half, :].rearrange("p (h d) -> p h d", d=DIFF_D)
            t = yield from self.head_norm(heads, 2 * DIFF_H, DIFF_D, small(gain), got[name][half])
            yield
            n = DIFF_D // 2
            got[name][half] = self.rotate(heads[:, :, 0:n], heads[:, :, n:], rope(0, half, 0, n, 2 * DIFF_H), rope(1, half, 0, n, 2 * DIFF_H),
                                          [t, self.rope_ready])

        def memory_keys():
            for half in range(HALVES):
                z = ck[:, half, :].rearrange("p (h d) -> p h d", h=CROSS_H)
                got["ck"][half] = yield from self.head_norm(z, CROSS_H, CROSS_D, small("cross_k_gain_2"), got["ck"][half])
            yield from turn_heads("ckt", lambda half, c: ck[:, half, c * P:(c + 1) * P], ckt, CROSS_H, got["ck"], mem_turned)

        def cross_queries():
            yield from need("xq", ("mkt", "used"))
            for half in range(HALVES):
                z = xq[:, half, :].rearrange("p (h d) -> p h d", h=CROSS_H)
                got["xq"][half] = yield from self.head_norm(z, CROSS_H, CROSS_D, small("cross_q_gain_2"), got["xq"][half])
            yield from turn_heads("cqt", lambda half, c: xq[:, half, c * P:(c + 1) * P], cqt, CROSS_H, got["xq"], got["mkt", "used"])

        def diff_operand(name, z, zt, gain):
            yield from need(name)
            for half in range(HALVES):
                yield from diff_part(name, z, half, gain)
                yield
            yield from turn_heads(name + "t", lambda half, c: z[:, half, c * P:(c + 1) * P], zt, DC, got[name])

        def latent():
            n = MLA_ROPE // 2
            yield from need("cq", "ckv")
            kr_ready = [None, None]
            for half in range(HALVES):
                t_q = self.wide_norm(low[:, half, 0:MLA_QL], MLA_QL, small("mla_qa_gain_2"), got["cq"][half])
                yield
                t_kv = self.wide_norm(low[:, half, ckv_at:kr], MLA_KVL, small("mla_kva_gain_2"), got["ckv"][half])
                yield
                z = low[:, half:half + 1, kr:kr + MLA_ROPE]
                kr_ready[half] = self.rotate(z[:, :, 0:n], z[:, :, n:2 * n], rope(0, half, DIFF_D // 2, n, 1), rope(1, half, DIFF_D // 2, n, 1),
                                             [got["ckv"][half], self.rope_ready])
                for place, c0, m, t in ((0, 0, MLA_QL // P, t_q), (MLA_QL // P, ckv_at, MLA_KVL // P, t_kv)):
                    yield
                    self.turn_part(lambda h, c, c0=c0: low[:, h, c0 + c * P:c0 + (c + 1) * P], low_t, half,
                                   [(place + c, c) for c in range(m)], t, None)
            got["low_t"] = kr_ready, pe.last()
            yield from need("mq")
            for half in range(HALVES):
                z = mq[:, half, :].rearrange("p (h d) -> p h d", d=MLA_QK)
                t = self.rotate(z[:, :, MLA_NOPE:MLA_NOPE + n], z[:, :, MLA_NOPE + n:], rope(0, half, DIFF_D // 2, n, MLA_H),
                                rope(1, half, DIFF_D // 2, n, MLA_H), [got["mq"][half], self.rope_ready])
                yield
                got["mq"][half] = yield from self.head_norm(z, MLA_H, MLA_QK, small("mla_q_gain_2"), [t, got["mq"][half]])
                yield
            yield from turn_heads("mqt", lambda half, h: mq[:, half, h * MLA_QK:(h + 1) * MLA_QK], mqt, MLA_H, got["mq"], mem_t.free)

        def latent_keys():
            yield from need("kv")
            kr_ready, low_turned = got["low_t"]
            kcat_ready = [None, None]
            for half in range(HALVES):
                zk = kcat[:, half, :].rearrange("p (h d) -> p h d", d=MLA_QK)
                dve.wait(got["kv"][half], kr_ready[half], low_turned)
                dve.do(dve.e.tensor_copy(zk[:, :, 0:MLA_NOPE], kv[:, half, :].rearrange("p (h d) -> p h d", d=per_kv)[:, :, 0:MLA_NOPE]))
                t = dve.do(dve.e.tensor_copy(zk[:, :, MLA_NOPE:], low[:, half:half + 1, kr:kr + MLA_ROPE].to_broadcast([P, MLA_H, MLA_ROPE])))
                kcat_ready[half] = yield from self.head_norm(zk, MLA_H, MLA_QK, small("mla_k_gain_2"), t)
                yield
            yield from turn_heads("mkt", lambda half, h: kcat[:, half, h * MLA_QK:(h + 1) * MLA_QK], mkt, MLA_H, kcat_ready, mem_t.free)
            got["mkt", "used"] = pe.last()

        def outputs():
            yield from need("mqt", "mkt")
            yield from attend("mla", 4, divided("mla", o_mla, MLA_V, 4, 2 * DIFF_H))
            mc_t.free = pe.last()
            yield from need("qt", "kt", "v")
            self.turn_all(lambda half: o_mla[:, 1 - half, :], mc_t, 4, [o_ready["mla"]] * 2)
            yield from attend("diff", 2, diff_done)
            diff_t.free = pe.last()
            yield from need("cqt")
            yield from together(cross_outputs(), diff_outputs())

        def cross_outputs():
            yield from attend("cross", 2, divided("cross", o_cross, CROSS_D, 2, 2 * DIFF_H + MLA_H))
            self.turn_all(lambda half: o_cross[:, 1 - half, :], mc_t, 4, [o_ready["cross"]] * 2, first=4)

        def diff_outputs():
            for half in range(HALVES):
                z = o_diff[:, 1 - half, :].rearrange("p (h d) -> p h d", h=DIFF_H)
                t = yield from self.head_norm(z, DIFF_H, 2 * DIFF_D, small("diff_out_gain_2"), o_ready["diff"], 1.0 - lam_init)
                yield from self.pause(2)
                for c0 in range(0, DC, 4):
                    self.turn_part(lambda h, c: o_diff[:, 1 - h, c * P:(c + 1) * P], diff_t, half, [(c0 + c, c0 + c) for c in range(4)], t, diff_t.free)
                    yield

        o_ready = {"cross": [], "mla": [], "diff": []}

        def heads_of(kind):
            if kind == "cross":
                for h in range(CROSS_H):
                    yield dict(q=lambda half, h=h: cqt[:, h, half, :], k=ckt[:, h, :],
                               v=lambda kh, h=h: cv[:, kh, h * CROSS_D:(h + 1) * CROSS_D], dv=CROSS_D, scale=CROSS_D ** -0.5,
                               bias=None, ready=[got["cqt"], got["ckt"], got["cv"]], at=2 * DIFF_H + MLA_H + h)
            if kind == "mla":
                for h in range(MLA_H):
                    yield dict(q=lambda half, h=h: mqt[0:MLA_QK, h, half * P:(half + 1) * P], k=mkt[0:MLA_QK, h, :],
                               v=lambda kh, h=h: kv[:, kh, h * per_kv + MLA_NOPE:(h + 1) * per_kv], dv=MLA_V, scale=MLA_QK ** -0.5,
                               bias=self.causal[:, :], ready=[got["mqt"], got["mkt"], got["kv"]], at=2 * DIFF_H + h)
            if kind == "diff":
                for h in range(DIFF_H):
                    for m in range(2):
                        r = slice(m * DIFF_D, (m + 1) * DIFF_D)
                        yield dict(q=lambda half, h=h, r=r: qt[r, h, half * P:(half + 1) * P], k=kt[r, h, :],
                                   v=lambda kh, h=h: v[:, kh, h * 2 * DIFF_D:(h + 1) * 2 * DIFF_D], dv=2 * DIFF_D, scale=DIFF_D ** -0.5,
                                   bias=self.causal[:, :], ready=[got["qt"], got["kt"], got["v"]], at=2 * h + m)

        def attend(kind, per_bank, done):
            heads = list(heads_of(kind))
            for h in heads:
                h["nmax"], h["den"] = nmax[:, h["at"], :], den[:, h["at"], :]
                h["causal"] = h["bias"] is not None
                h["bias_ready"], h["bias_used"] = (lambda: None), (lambda t: None)
            yield from self.attention(heads, per_bank, done)

        def divided(kind, dst, dv, per_bank, first):
            def done(bank, h0, t):
                r = self.stat(2 * per_bank)
                rv = r.rearrange("p (s h) -> p s h", s=2)
                dve.wait(t)
                dve.wait(act.last())
                u = dve.do(dve.e.reciprocal(rv, den[:, first + h0:first + h0 + per_bank, :].rearrange("p h s -> p s h")))
                dve.wait(u)
                view = bank.rearrange("p (s h d) -> p s h d", s=2, h=per_bank)
                out = dst[:, :, h0 * dv:(h0 + per_bank) * dv].rearrange("p s (h d) -> p s h d", h=per_bank)
                rb = r.rearrange("p (s h o) -> p s h o", s=2, o=1).to_broadcast([P, 2, per_bank, dv])
                u = dve.do(dve.e.tensor_tensor(out, view, rb, ALU.mult))
                self.banks.give(bank, u)
                o_ready[kind].append(u)
            return done

        def diff_done(bank, h0, t):
            r = self.stat(4)
            rv = r.rearrange("p (s m) -> p s m", s=2)
            dve.wait(t, act.last())
            u = dve.do(dve.e.reciprocal(rv, den[:, h0:h0 + 2, :].rearrange("p m s -> p s m")))
            dve.wait(u, lam_ready)
            u = dve.do(dve.e.tensor_scalar(rv[:, :, 1:2], rv[:, :, 1:2], lam[:, 5:6], None, ALU.mult))
            tmp, free = self.tmp.take()
            dve.wait(u, free)
            view = bank.rearrange("p (s m d) -> p s m d", s=2, m=2)
            tv = tmp[:, :].rearrange("p (s m d) -> p s m d", s=2, m=2)
            rb = r.rearrange("p (s m o) -> p s m o", s=2, o=1).to_broadcast([P, 2, 2, 2 * DIFF_D])
            u = dve.do(dve.e.tensor_tensor(tv, view, rb, ALU.mult))
            self.banks.give(bank, u)
            dve.wait(u)
            c = (h0 // 2) * 2 * DIFF_D
            u = dve.do(dve.e.tensor_tensor(o_diff[:, :, c:c + 2 * DIFF_D], tv[:, :, 0, :], tv[:, :, 1, :], ALU.subtract))
            self.tmp.give(tmp, u)
            o_ready["diff"].append(u)

        side = together(latent(), latent_keys(), memory_keys(), diff_operand("q", q, qt, "diff_q_gain_2"), diff_operand("k", k, kt, "diff_k_gain_2"),
                        cross_queries(), outputs())
        self.drive(projections(), side, steps=2, finish=False)
        merged = self.place("mx_merged" + L, 56, [P, HALVES, D])
        gates_ready = {}
        for g, tile in enumerate(gates):
            act.wait(got["gate", g])
            for half in range(HALVES):
                gates_ready[g, half] = act.do(act.e.activation(tile[:, half, :], tile[:, half, :], ACT.Sigmoid))

        merged_ready = {}
        self.xt.ready, self.xt.scale = {}, [(None, None)] * HALVES
        merged_free = self.xt.free

        def branch(xt, rows, first):
            while any((half, first + c) not in xt.ready for half in range(HALVES) for c in range(rows // P)):
                yield
            return (yield from self.block(xt, rows, BLOCK, first))

        def turn_merged(c):
            for half in range(HALVES):
                self.turn_part(lambda h, s: merged[:, h, s * P:(s + 1) * P], self.xt, half, [(4 * c + j, 4 * c + j) for j in range(4)],
                               merged_ready[half, c], merged_free)

        def merge():
            for n, (g, xt, rows, first) in enumerate(((1, mc_t, MLA_H * MLA_V, 0), (2, mc_t, CROSS_H * CROSS_D, 4), (0, diff_t, D, 0))):
                for c, (c0, m) in enumerate(column_blocks(D)):
                    banks, ts = yield from branch(xt, rows, first)
                    for half in range(HALVES):
                        total = merged[:, half, c0:c0 + m]
                        gate = gates[g][:, half, c0:c0 + m]
                        dve.wait(ts[half], gates_ready[g, half])
                        if n == 0:
                            merged_ready[half, c] = dve.do(dve.e.tensor_tensor(total, banks[half], gate, ALU.mult))
                            self.banks.give(banks[half], merged_ready[half, c])
                            continue
                        tmp, free = self.tmp.take()
                        dve.wait(free)
                        u = dve.do(dve.e.tensor_tensor(tmp[:, 0:m], banks[half], gate, ALU.mult))
                        self.banks.give(banks[half], u)
                        dve.wait(merged_ready[half, c], u)
                        merged_ready[half, c] = dve.do(dve.e.tensor_tensor(total, total, tmp[:, 0:m], ALU.add))
                        self.tmp.give(tmp, merged_ready[half, c])
        self.drive(merge(), side, 1)
        turn_merged(0)
        turn_merged(1)
        self.tok_free = [pe.last()] * HALVES
        self.drive(self.last_plain(self.xt, D))

    def store(self, out):
        dma = DmaSlot(self.nc, "out", None)
        for half in range(HALVES):
            for c in range(2):
                self.pending(half, c)
            self.sync.wait(self.x_ready[half], self.masks_ready)
            t = dma.filled(self.sync.e.dma_start(out[0, half * P:(half + 1) * P, :], self.x[:, half, :]))
        self.sync.wait(t)


STAGES = [("ffn", 0, 0), ("dilated", 0, 0), ("ffn", 0, 1), ("ffn", 1, 0), ("retention", 1, 0), ("ffn", 1, 1),
          ("mix", 0, 0), ("mlp", 0, 0), ("mix", 1, 0), ("mlp", 1, 0)]


def program(nc, a, out, stages=STAGES):
    k = Kernel(nc, a, stages)
    for n, (kind, i, j) in enumerate(stages):
        k.act_share = 3 if kind == "mix" else 2
        k.weights.share = dict(dilated=3, retention=3, mix=2).get(kind, 0)
        k.following = stages[n + 1] if n + 1 < len(stages) else None
        dict(ffn=k.ffn, mlp=k.mlp, dilated=k.dilated, retention=k.retention, mix=k.mix)[kind](i, j)
    k.store(out)


INPUTS = ["x", "norm_gains", "ffn_w_gate", "ffn_w_up", "ffn_w_down", "attn_w_in", "attn_w_out", "rel_bias", "ret_w_in",
          "ret_w_out", "ret_decay_logit", "mem_2", "positions_2", "g_mix_2", "w_in_2", "b_gate_2", "diff_q_gain_2",
          "diff_k_gain_2", "diff_lambda_2", "diff_out_gain_2", "w_diff_o_2", "mla_qa_gain_2", "w_mla_qb_2",
          "mla_kva_gain_2", "w_mla_kvb_2", "mla_q_gain_2", "mla_k_gain_2", "w_mla_o_2", "mem_gain_2", "w_mem_kv_2",
          "cross_q_gain_2", "cross_k_gain_2", "w_cross_o_2", "w_out_2", "g_mlp_2", "w_mlp1_2", "w_mlp2_2"]


def kernel(**inputs):
    import concourse.bacc as bacc
    from concourse.bass_utils import run_bass_kernel_spmd

    nc = bacc.Bacc("TRN2", target_bir_lowering=False, num_devices=1)
    arrays = {name: np.ascontiguousarray(inputs[name]) for name in INPUTS}
    arrays.update(constants())
    aps, sent = {}, {}
    for name, v in arrays.items():
        sent["in_" + name] = v
        aps[name] = nc.dram_tensor("in_" + name, v.shape, mybir.dt.from_np(v.dtype), kind="ExternalInput").ap()
    out = nc.dram_tensor("out_x", (1, SEQ, D), F32, kind="ExternalOutput").ap()
    program(nc, aps, out)
    r = run_bass_kernel_spmd(nc, [sent], core_ids=[0])
    return r.results[0]["out_x"]
```
